# Optimizing a Trainium2 kernel written in Bass

```python
import jax, jax.numpy as jnp
from jax import lax
import numpy as np

D_MODEL = 1024
BATCH = 1
SEQ = 256
DEPTH = 2

MIX_WIDTH = D_MODEL
A_HEADS = 8
A_HEAD_DIM = 64
IDX_HEADS = 8
IDX_DIM = 64
TOPK_MAX = 256
Q_BLOCK = 128
B_HEADS = 4
B_KEY_DIM = 64
B_VAL_DIM = 128
GATE_RANK = 16
GATE_TAU = 16.0
CHUNK = 64
D_FF = 2816
N_EXPERTS = 8
TOP_K_EXPERTS = 2
MOE_BLOCK = 256
N_DENSE = (DEPTH + 1) // 2
N_MOE = DEPTH // 2
DN_ALPHA = (2 * DEPTH) ** 0.25
DN_BETA = (8 * DEPTH) ** -0.25
NORM_EPS = 1e-5

A_Q_W = A_HEADS * A_HEAD_DIM
A_K_W = A_HEAD_DIM
A_V_W = A_HEAD_DIM
I_Q_W = IDX_HEADS * IDX_DIM
I_K_W = IDX_DIM
I_W_W = IDX_HEADS
B_Q_W = B_HEADS * B_KEY_DIM
B_K_W = B_HEADS * B_KEY_DIM
B_V_W = B_HEADS * B_VAL_DIM
B_G_W = B_HEADS * B_VAL_DIM
B_A_W = GATE_RANK
SEG_WIDTHS = (A_Q_W, A_K_W, A_V_W, I_Q_W, I_K_W, I_W_W, B_Q_W, B_K_W, B_V_W, B_G_W, B_A_W)
VALUE_SEGS = (2, 8)
PROJ_WIDTH = A_Q_W + A_K_W + A_V_W + I_Q_W + I_K_W + I_W_W + B_Q_W + B_K_W + B_V_W + B_G_W + B_A_W

kernel_name = 'hybrid_dsa_gla_deepnorm_moe'

def _split_points():
    pts, acc = [], 0
    for w in SEG_WIDTHS[:-1]:
        acc += w
        pts.append(acc)
    return pts

def layer_norm(x, g, b):
    xf = x.astype(jnp.float32)
    mu = jnp.mean(xf, axis=-1, keepdims=True)
    var = jnp.mean(jnp.square(xf - mu), axis=-1, keepdims=True)
    y = (xf - mu) * lax.rsqrt(var + NORM_EPS) * g.astype(jnp.float32) + b.astype(jnp.float32)
    return y.astype(x.dtype)

def rms_norm(x, g):
    xf = x.astype(jnp.float32)
    y = xf * lax.rsqrt(jnp.mean(jnp.square(xf), axis=-1, keepdims=True) + NORM_EPS)
    return (y * g.astype(jnp.float32)).astype(x.dtype)

def alibi_slopes(n):
    return jnp.exp2(-8.0 * jnp.arange(1, n + 1, dtype=jnp.float32) / n)

def dsa_attention(q, k, v, q_idx, k_idx, w_idx):
    bsz, L = q.shape[0], q.shape[1]
    k_top = min(TOPK_MAX, L // 4)
    n_blocks = L // Q_BLOCK
    slopes = alibi_slopes(A_HEADS)
    key_pos = jnp.arange(L)
    scale = A_HEAD_DIM ** -0.5
    idx_scale = IDX_DIM ** -0.5
    k_idx_f = k_idx.astype(jnp.float32)
    gather = jax.vmap(lambda table, ids: table[ids])

    def block(i):
        t0 = i * Q_BLOCK
        qb = lax.dynamic_slice_in_dim(q, t0, Q_BLOCK, axis=1)
        qib = lax.dynamic_slice_in_dim(q_idx, t0, Q_BLOCK, axis=1)
        wib = lax.dynamic_slice_in_dim(w_idx, t0, Q_BLOCK, axis=1)
        qpos = t0 + jnp.arange(Q_BLOCK)
        s_idx = jnp.einsum('bthd,bsd->bths', qib.astype(jnp.float32), k_idx_f) * idx_scale
        scores = jnp.einsum('bth,bths->bts', wib.astype(jnp.float32), jax.nn.relu(s_idx))
        causal = key_pos[None, :] <= qpos[:, None]
        scores = jnp.where(causal[None], scores, -jnp.inf)
        _, sel = lax.top_k(scores, k_top)
        k_sel = gather(k, sel)
        v_sel = gather(v, sel)
        dist = (qpos[None, :, None] - sel).astype(jnp.float32)
        logits = jnp.einsum('bthd,btkd->bthk', qb, k_sel).astype(jnp.float32) * scale
        logits = logits - slopes[None, None, :, None] * dist[:, :, None, :]
        logits = jnp.where((dist >= 0)[:, :, None, :], logits, -jnp.inf)
        p = jax.nn.softmax(logits, axis=-1)
        return jnp.einsum('bthk,btkd->bthd', p.astype(v.dtype), v_sel)

    outs = lax.map(block, jnp.arange(n_blocks))
    return outs.transpose(1, 0, 2, 3, 4).reshape(bsz, L, A_HEADS * A_HEAD_DIM)

def gla(q, k, v, log_a):
    bsz, L = q.shape[0], q.shape[1]
    nc = L // CHUNK

    def to_chunks(z):
        return z.astype(jnp.float32).reshape(bsz, nc, CHUNK, B_HEADS, -1).transpose(1, 0, 3, 2, 4)

    qc = to_chunks(q) * (B_KEY_DIM ** -0.5)
    kc, vc, gc = to_chunks(k), to_chunks(v), to_chunks(log_a)
    tri = jnp.tril(jnp.ones((CHUNK, CHUNK), dtype=bool))

    def step(state, inp):
        qi, ki, vi, gi = inp
        b = jnp.cumsum(gi, axis=2)
        b_last = b[:, :, -1:, :]
        inter = jnp.einsum('bhtd,bhde->bhte', qi * jnp.exp(b), state)
        diff = b[:, :, :, None, :] - b[:, :, None, :, :]
        decay = jnp.exp(jnp.where(tri[None, None, :, :, None], diff, -jnp.inf))
        attn = jnp.einsum('bhtd,bhsd,bhtsd->bhts', qi, ki, decay)
        out = inter + jnp.einsum('bhts,bhse->bhte', attn, vi)
        new_state = jnp.exp(b_last)[:, :, 0, :, None] * state + \
            jnp.einsum('bhsd,bhse->bhde', ki * jnp.exp(b_last - b), vi)
        return new_state, out

    init = jnp.zeros((bsz, B_HEADS, B_KEY_DIM, B_VAL_DIM), jnp.float32)
    _, outs = lax.scan(step, init, (qc, kc, vc, gc))
    return outs.transpose(1, 0, 3, 2, 4).reshape(bsz, L, B_HEADS, B_VAL_DIM).astype(q.dtype)

def hybrid_mixer(h, w_in, w_a2, b_a, gla_g, w_out):
    bsz, L, _ = h.shape
    proj = h @ w_in
    aq, ak, av, iq, ik, iw, bq, bk, bv, bg, ba = jnp.split(proj, _split_points(), axis=-1)
    y_a = dsa_attention(
        aq.reshape(bsz, L, A_HEADS, A_HEAD_DIM), ak, av,
        iq.reshape(bsz, L, IDX_HEADS, IDX_DIM), ik, iw * (IDX_HEADS ** -0.5))
    log_a = jax.nn.log_sigmoid((ba @ w_a2 + b_a).astype(jnp.float32)) / GATE_TAU
    o = gla(bq.reshape(bsz, L, B_HEADS, B_KEY_DIM), bk.reshape(bsz, L, B_HEADS, B_KEY_DIM),
            bv.reshape(bsz, L, B_HEADS, B_VAL_DIM), log_a.reshape(bsz, L, B_HEADS, B_KEY_DIM))
    o = rms_norm(o, gla_g) * jax.nn.silu(bg.reshape(bsz, L, B_HEADS, B_VAL_DIM))
    y = jnp.concatenate([y_a, o.reshape(bsz, L, B_HEADS * B_VAL_DIM)], axis=-1)
    return y @ w_out

def swiglu(h, w_gate, w_up, w_down):
    return (jax.nn.silu(h @ w_gate) * (h @ w_up)) @ w_down

def moe_swiglu(h, w_router, b_router, we_gate, we_up, we_down):
    bsz, L, d = h.shape
    n_tok = bsz * L
    xf = h.reshape(n_tok, d)
    logits = (xf @ w_router + b_router).astype(jnp.float32)
    top_val, top_idx = lax.top_k(logits, TOP_K_EXPERTS)
    gates = jax.nn.softmax(top_val, axis=-1)
    n_assign = n_tok * TOP_K_EXPERTS
    e_flat = top_idx.reshape(-1)
    tok_flat = jnp.repeat(jnp.arange(n_tok, dtype=jnp.int32), TOP_K_EXPERTS)
    g_flat = gates.reshape(-1)
    order = jnp.argsort(e_flat)
    e_sorted = e_flat[order]
    counts = jnp.bincount(e_flat, length=N_EXPERTS)
    padded = ((counts + MOE_BLOCK - 1) // MOE_BLOCK) * MOE_BLOCK
    start = jnp.cumsum(counts) - counts
    pstart = jnp.cumsum(padded) - padded
    pend = pstart + padded
    dest = pstart[e_sorted] + (jnp.arange(n_assign) - start[e_sorted])
    n_blocks = -(-n_assign // MOE_BLOCK) + N_EXPERTS
    n_rows = n_blocks * MOE_BLOCK
    buf_tok = jnp.zeros((n_rows,), jnp.int32).at[dest].set(tok_flat[order])
    buf_gate = jnp.zeros((n_rows,), jnp.float32).at[dest].set(g_flat[order])
    blk_expert = jnp.minimum(
        jnp.searchsorted(pend, jnp.arange(n_blocks) * MOE_BLOCK, side='right'), N_EXPERTS - 1)

    def run_block(args):
        toks, gts, e = args
        y = swiglu(xf[toks], we_gate[e], we_up[e], we_down[e])
        return y * gts[:, None].astype(y.dtype)

    yb = lax.map(run_block, (buf_tok.reshape(n_blocks, MOE_BLOCK),
                             buf_gate.reshape(n_blocks, MOE_BLOCK), blk_expert))
    out = jax.ops.segment_sum(yb.reshape(n_rows, d), buf_tok, num_segments=n_tok)
    return out.reshape(bsz, L, d)

def setup_inputs(seed: int = 0) -> dict:
    key = jax.random.key(seed)
    ks = jax.random.split(key, 20)
    f32 = jnp.float32
    nrm = lambda k, shape: jax.random.normal(k, shape, f32)
    col_scale = jnp.concatenate([
        jnp.full((w,), DN_BETA if i in VALUE_SEGS else 1.0, f32) for i, w in enumerate(SEG_WIDTHS)])
    return {
        'x': nrm(ks[0], (BATCH, SEQ, D_MODEL)),
        'c': nrm(ks[1], (BATCH, D_MODEL)),
        'w_in': nrm(ks[2], (DEPTH, D_MODEL, PROJ_WIDTH)) * (D_MODEL ** -0.5) * col_scale,
        'w_a2': nrm(ks[3], (DEPTH, GATE_RANK, B_HEADS * B_KEY_DIM)) * (GATE_RANK ** -0.5),
        'b_a': 0.1 * nrm(ks[4], (DEPTH, B_HEADS * B_KEY_DIM)),
        'gla_norm_g': 1.0 + 0.1 * nrm(ks[5], (DEPTH, B_VAL_DIM)),
        'w_out': nrm(ks[6], (DEPTH, MIX_WIDTH, D_MODEL)) * (MIX_WIDTH ** -0.5) * DN_BETA,
        'w_mod': nrm(ks[7], (DEPTH, D_MODEL, 6 * D_MODEL)) * (D_MODEL ** -0.5) * 0.1,
        'b_mod': 0.01 * nrm(ks[8], (DEPTH, 6 * D_MODEL)),
        'ln_g': 1.0 + 0.1 * nrm(ks[9], (DEPTH, 2, D_MODEL)),
        'ln_b': 0.02 * nrm(ks[10], (DEPTH, 2, D_MODEL)),
        'ffn_w_gate': nrm(ks[11], (N_DENSE, D_MODEL, D_FF)) * (D_MODEL ** -0.5),
        'ffn_w_up': nrm(ks[12], (N_DENSE, D_MODEL, D_FF)) * (D_MODEL ** -0.5),
        'ffn_w_down': nrm(ks[13], (N_DENSE, D_FF, D_MODEL)) * (D_FF ** -0.5) * DN_BETA,
        'w_router': nrm(ks[14], (N_MOE, D_MODEL, N_EXPERTS)) * (D_MODEL ** -0.5),
        'b_router': 0.01 * nrm(ks[15], (N_MOE, N_EXPERTS)),
        'moe_w_gate': nrm(ks[16], (N_MOE, N_EXPERTS, D_MODEL, D_FF)) * (D_MODEL ** -0.5),
        'moe_w_up': nrm(ks[17], (N_MOE, N_EXPERTS, D_MODEL, D_FF)) * (D_MODEL ** -0.5),
        'moe_w_down': nrm(ks[18], (N_MOE, N_EXPERTS, D_FF, D_MODEL)) * (D_FF ** -0.5) * DN_BETA,
    }

def reference(x, c, w_in, w_a2, b_a, gla_norm_g, w_out, w_mod, b_mod, ln_g, ln_b,
              ffn_w_gate, ffn_w_up, ffn_w_down, w_router, b_router,
              moe_w_gate, moe_w_up, moe_w_down):
    c_act = jax.nn.silu(c)
    for l in range(DEPTH):
        mod = (c_act @ w_mod[l] + b_mod[l])[:, None, :]
        sh1, sc1, g1, sh2, sc2, g2 = jnp.split(mod, 6, axis=-1)
        h = x * (1.0 + sc1) + sh1
        y = hybrid_mixer(h, w_in[l], w_a2[l], b_a[l], gla_norm_g[l], w_out[l])
        x = layer_norm(DN_ALPHA * x + (1.0 + g1) * y, ln_g[l, 0], ln_b[l, 0])
        h = x * (1.0 + sc2) + sh2
        if l % 2 == 0:
            j = l // 2
            y = swiglu(h, ffn_w_gate[j], ffn_w_up[j], ffn_w_down[j])
        else:
            j = l // 2
            y = moe_swiglu(h, w_router[j], b_router[j], moe_w_gate[j], moe_w_up[j], moe_w_down[j])
        x = layer_norm(DN_ALPHA * x + (1.0 + g2) * y, ln_g[l, 1], ln_b[l, 1])
    return x


_drawn_inputs = setup_inputs


def setup_inputs(seed=0):
    import zlib

    import numpy as np

    out = dict(_drawn_inputs(seed))
    spreads = {}
    factors = {'b_a': 4.067, 'b_mod': 2.701, 'b_router': 21.744}
    for name, (base, spread) in spreads.items():
        noise = np.random.default_rng([zlib.crc32(name.encode()), seed]).standard_normal(out[name].shape)
        drawn = base * np.exp(spread * noise) if base else spread * noise
        out[name] = __import__('jax').numpy.asarray(drawn.astype(out[name].dtype))
    for name, factor in factors.items():
        out[name] = (out[name] * factor).astype(out[name].dtype)
    return out
```

```python
from contextlib import ExitStack

import concourse.bass as bass
from concourse import mybir

F32 = mybir.dt.float32
F32R = mybir.dt.float32r
I32 = mybir.dt.int32
ALU = mybir.AluOpType
ACT = mybir.ActivationFunctionType
AX = mybir.AxisListType

P = 128
D = 1024
KT = D // P
T = 256
TT = T // P
DEPTH = 2
A_HEADS = 8
TOPK = min(256, T // 4)
B_HEADS = 4
B_DV = 128
RANK = 16
D_FF = 2816
FC = 256
STEPS = D_FF // FC
NE = 8
UNITC = 256
ALPHA = (2 * DEPTH) ** 0.25
EPS = 1e-5
NEG = -1.0e30
FILL = -1.0e38
TAKEN = -3.0e38
SQ = 64 ** -0.5
BLK = 32
NBLK = P // BLK

AQ, AK, AV, IQ, IK, IW, BQ, BK, BV, BG, BA = 0, 512, 576, 640, 1152, 1216, 1224, 1480, 1736, 2248, 2760
U_IQ0, U_IQ1, U_IKW, U_AQ0, U_AQ1, U_AKV, U_BQ, U_BK, U_BA, U_BV0, U_BV1, U_BG0, U_BG1 = range(13)
W_IN_UNITS = [(IQ, 256), (IQ + 256, 256), (IK, 72), (AQ, 256), (AQ + 256, 256), (AK, 128), (BQ, 256),
              (BK, 256), (BA, RANK), (BV, 256), (BV + 256, 256), (BG, 256), (BG + 256, 256)]
NIN = len(W_IN_UNITS)
NU = NIN + D // UNITC
MOD_ROWS = [(l, a, k) for l in range(DEPTH) for a in range(0 if l else 2, 6) for k in range(KT)]
ROWS_L0 = 4 * KT
ROWS_AT_UNIT = {1: 3, 2: 3, 3: 3, 4: 3, 5: 4, 10: 3, 11: 3, 12: 3, 13: 3, 14: 4}
ROWS_STEP = 4
MOD_AT_STEP = {2 * a + 1: a for a in range(5)}
HEAD_GROUPS = [(0, range(0, 4), 128), (0, range(4, 8), 128)] + [(1, range(2 * g, 2 * g + 2), 256) for g in range(4)]
NG = len(HEAD_GROUPS)


def hybrid_decoder(nc, x, c, w_in, w_a2, b_a, gla_norm_g, w_out, w_mod, b_mod, ln_g, ln_b,
                   ffn_w_gate, ffn_w_up, ffn_w_down, w_router, b_router,
                   moe_w_gate, moe_w_up, moe_w_down, out):
    ctx = ExitStack()
    with ctx:
        top = [16640]

        def place(name, shape, dt=F32, at=None):
            size = 4
            for n in shape[1:]:
                size *= n
            size = (size + 31) // 32 * 32
            if at is None:
                at = top[0]
                top[0] += size
            return nc.alloc_sbuf_tensor_at(name, shape, dt, offset=at)

        def sem(name):
            return ctx.enter_context(nc.semaphore(name))

        x_sb = place("x_sb", [P, TT, D])
        hT_H = place("hT_H", [P, KT, T], F32R)
        hT_L = place("hT_L", [P, KT, T], F32R)
        hfull_at = top[0]
        hfull = place("hfull", [P, KT, T])
        ycat_at = top[0]
        ycat = place("ycat", [P, TT, D])
        rows_at = top[0]
        g_row = place("g_row", [P, D])
        lng_row = place("lng_row", [P, D])
        lnb_row = place("lnb_row", [P, D])
        hidT_at = top[0]
        hidT_H = place("hidT_H", [P, 2, 2, P], F32R)
        hidT_L = place("hidT_L", [P, 2, 2, P], F32R)
        hid = place("hid", [P, 2, FC])
        silu_g = place("silu_g", [P, 2, FC])
        ident = place("ident", [P, P])
        ones = place("ones", [P, T])
        upper = place("upper", [P, P])
        upper_eq = place("upper_eq", [P, P])
        dist = place("dist", [P, T])
        ahead = place("ahead", [P, T])
        slot_id = place("slot_id", [P, P])
        rev8 = place("rev8", [P, NE])
        half_neg = place("half_neg", [P, 8])
        stage = place("stage", [P, P])
        cols = place("cols", [P, P])
        modT = place("modT", [P, DEPTH * 48])
        c_act = place("c_act", [P, KT])
        stats = place("stats", [P, TT, 2, 6])
        mv = place("mv", [P, TT, 2])
        veps = place("veps", [P, TT])
        rstd = place("rstd", [P, TT])
        iw = place("iw", [P, TT, 8])
        top8 = place("top8", [P, 8])
        nmax = place("nmax", [P, TT, A_HEADS])
        rsum = place("rsum", [P, TT, A_HEADS])
        rinv = place("rinv", [P, TT, A_HEADS])
        ssq = place("ssq", [P, TT, B_HEADS])
        rms = place("rms", [P, TT, B_HEADS])
        gnorm = place("gnorm", [P, B_DV])
        nb127 = place("nb127", [P, 2])
        wr = place("wr", [P, KT, NE])
        br_row = place("br_row", [P, NE])
        raw_g0 = place("raw_g0", [P, KT, FC])
        raw_u0 = place("raw_u0", [P, KT, FC])
        gu_H0 = place("gu_H0", [P, KT, 2 * FC], F32R)
        gu_L0 = place("gu_L0", [P, KT, 2 * FC], F32R)
        over = top[0]
        raw_g1 = place("raw_g1", [P, KT, FC])
        raw_u1 = place("raw_u1", [P, KT, FC])
        raw_d0 = place("raw_d0", [P, 2, D])
        raw_d1 = place("raw_d1", [P, 2, D])
        d_H = place("d_H", [P, 2, D], F32R)
        d_L = place("d_L", [P, 2, D], F32R)
        gu_H1 = place("gu_H1", [P, KT, 2 * FC], F32R)
        gu_L1 = place("gu_L1", [P, KT, 2 * FC], F32R)
        end = top[0]
        raw_g, raw_u, raw_d = [raw_g0, raw_g1], [raw_u0, raw_u1], [raw_d0, raw_d1]
        gu_H, gu_L = [gu_H0, gu_H1], [gu_L0, gu_L1]
        top[0] = over
        aqT = place("aqT", [P, 4, T])
        iqT = place("iqT", [P, 4, T])
        akP = place("akP", [P, 2, T])
        ikP = place("ikP", [P, 2, T])
        av = place("av", [P, TT, 64])
        bqT = place("bqT", [P, 2, T])
        bkT = place("bkT", [P, 2, T])
        baT = place("baT", [P, T])
        wa2 = place("wa2", [P, T])
        bT = place("bT", [P, 2, T])
        dec0 = place("dec0", [P, 2, T])
        dec1 = place("dec1", [P, 2, T])
        bv = place("bv", [P, TT, 512])
        sbg = place("sbg", [P, TT, 512])
        score0 = place("score0", [P, P])
        score1 = place("score1", [P, T])
        relu_a = place("relu_a", [P, 512])
        relu_b = place("relu_b", [P, 512])
        dsel0 = place("dsel0", [P, P])
        dsel1 = place("dsel1", [P, T])
        prob0 = place("prob0", [P, A_HEADS, P])
        prob1 = place("prob1", [P, A_HEADS, T])
        pT0 = place("pT0", [P, 8, P])
        kfac = place("kfac", [P, 2, 2, NBLK, P])
        qfP = place("qfP", [P, 2, 2, T])
        qxP = place("qxP", [P, 2, 2, P])
        kx = place("kx", [P, 2, P])
        at_sb = place("at_sb", [P, 3, 512])
        assert top[0] <= end, (top[0] - end)
        assert end <= 229344, end
        pT1 = place("pT1", [P, 16, P], at=hfull_at)
        top[0] = end
        one_G = place("one_G", [P, TT, P], F32R)
        one_S = place("one_S", [P, T], F32R)
        rank_tab = place("rank_tab", [P, TT, 2 * NE + 1])
        gate_tab = place("gate_tab", [P, TT, 2 * NE + 1])
        rt = [place(f"rt{i}", [P, TT, NE]) for i in range(10)]
        v2 = place("v2", [P, 6, TT])
        tick = place("tick", [P, 8])
        npass_f = place("npass_f", [P, 2])
        npass_i = place("npass_i", [P, 1], I32)
        assert top[0] <= 229344, top[0]
        spare_at = top[0]
        mod_first = place("mod_first", [P, KT, 2 * D], at=over)
        top[0] = spare_at
        mod_acc = [place(f"mod_acc{i}", [P, D]) for i in range(2)]
        assert top[0] <= 229344, top[0]
        mod_ring = [[place(f"mod_row{l}{i}", [P, D], at=(ycat_at if i >= 2 else hfull_at if l else hidT_at) + 4 * D * (i % 2))
                     for i in range(4)] for l in range(DEPTH)]

        score, dsel, prob, relu = [score0, score1], [dsel0, dsel1], [prob0, prob1], [relu_a, relu_b]
        xH0 = place("xH0", [P, D], F32R, at=rows_at)
        xH1 = place("xH1", [P, D], F32R, at=rows_at + 4096)
        xL0 = place("xL0", [P, D], F32R, at=rows_at + 8192)
        xL1 = place("xL1", [P, D], F32R, at=hfull_at + 4096)
        xH, xL = [xH0, xH1], [xL0, xL1]
        xg_full = place("xg_full", [P, KT, P], at=hfull_at)
        xgH = hT_H[:, 0:4, :].rearrange("p a b -> p (a b)").rearrange("p (k n) -> p k n", k=KT)
        xgL = hT_L[:, 0:4, :].rearrange("p a b -> p (a b)").rearrange("p (k n) -> p k n", k=KT)
        yH = hT_H[:, 4:8, :].rearrange("p a b -> p (a b)")
        yL = hT_L[:, 4:8, :].rearrange("p a b -> p (a b)")

        bank = [ctx.enter_context(nc.psum_tensor(f"bank{i}", [P, 512], F32)) for i in range(8)]

        s = {}
        for name in """const x_ld stage_ld small_ld rows_ld wa2_ld pads stageT cols_rd cact mod_sum row_rd mod_ps modT x_ln xT_ps hfull hT_H hT_L
            gdiag g_ps g_row wH wL proj evac idx_ps relu idxacc dve_chain act_chain pool_chain z_ps az decay bcum
            qe ke kx_e kfac_rd gla_in at_ps at_sb at_msk o_ps ssq rms lg_ps lg_sb nmax pexp rinv pt_ps pt_sb pv_ps ycat
            yT_ps yT_H yT_L mv rstd stored
            f_guH f_guL f_gu f_silu f_hid f_t f_tH f_tL f_dH f_dL f_d
            rt_ps lg8 expd sel rank_ps npass xsplit xsplitL zeros G xg_ps xg_full xg_H xg_L
            m_guH m_guL m_gu m_silu m_hid m_t m_tH m_tL m_dH m_dL m_d m_st m_S m_sc m_acc m_yH m_yL m_end""".split():
            s[name] = sem("s_" + name)
        mod_ld = [sem(f"s_mod_ld{i}") for i in range(KT)]
        row_ld = [sem(f"s_row_ld{i}") for i in range(4)]
        w_ld = [sem(f"s_w_ld{i}") for i in range(2)]
        f_ld = {k: [sem(f"s_f_ld_{k}{i}") for i in range(2)] for k in "gud"}
        m_ld = {k: [sem(f"s_m_ld_{k}{i}") for i in range(2)] for k in "gud"}

        block = ctx.enter_context(nc.Block())

        def unit_rows(u):
            n = sum(ROWS_AT_UNIT[v] for v in ROWS_AT_UNIT if v < u)
            return range(n, n + ROWS_AT_UNIT.get(u, 0))

        def step_rows(q):
            n = ROWS_L0 + ROWS_STEP * (q + 1)
            return range(n, n + ROWS_STEP)

        def mm3(out_ap, aH, aL, bH, bL, first, last):
            nc.tensor.matmul(out_ap, aH, bH, start=first, stop=False)
            nc.tensor.matmul(out_ap, aH, bL, start=False, stop=False)
            return nc.tensor.matmul(out_ap, aL, bH, start=False, stop=last)

        def unit_src(l, u):
            if u < NIN:
                a, n = W_IN_UNITS[u]
                return w_in[l, :, a:a + n].rearrange("(k p) f -> p k f", p=P), n
            a = (u - NIN) * UNITC
            return w_out[l, :, a:a + UNITC].rearrange("(k p) f -> p k f", p=P), UNITC

        wraw = [raw_g0, raw_u0]

        @block.sync
        def _(sp):
            for k in range(KT):
                sp.dma_start(mod_first[:, k, :], w_mod[0, k * P:(k + 1) * P, 0:2 * D]).then_inc(mod_ld[k], 16)
                if k >= KT - TT:
                    t = k - (KT - TT)
                    sp.dma_start(x_sb[:, t, :], x[0, t * P:(t + 1) * P, :]).then_inc(s["x_ld"], 16)

            def load_mod_rows(rows):
                for n in rows:
                    l, a, k = MOD_ROWS[n]
                    if n >= 4:
                        sp.wait_ge(s["row_rd"], n - 3)
                    else:
                        sp.wait_ge(s["mod_ps"], 1)
                    if n == ROWS_L0:
                        sp.wait_ge(s["hT_L"], 4)
                        sp.wait_ge(s["g_ps"], 4)
                    sp.dma_start(mod_ring[l][n % 4][:], w_mod[l, k * P:(k + 1) * P, a * D:(a + 1) * D])\
                        .then_inc(row_ld[n % 4], 16)

            def mixer_loads(l):
                for u in range(NU):
                    if u >= 2:
                        sp.wait_ge(s["wL"], l * NU + u - 1)
                    elif l:
                        sp.wait_ge(s["f_guL"], 2 * STEPS)
                    src, n = unit_src(l, u)
                    sp.dma_start(wraw[u % 2][:, :, 0:n], src).then_inc(w_ld[u % 2], 16)
                    if l == 0:
                        load_mod_rows(unit_rows(u))

            mixer_loads(0)

            def dense_gu(q):
                if q == 0:
                    sp.wait_ge(s["wL"], NU)
                elif q == 1:
                    sp.wait_ge(s["yT_L"], 4)
                else:
                    sp.wait_ge(s["f_guL"], 2 * (q - 1))
                f = slice(q * FC, (q + 1) * FC)
                sp.dma_start(raw_g[q % 2][:], ffn_w_gate[0, :, f].rearrange("(k p) f -> p k f", p=P)).then_inc(f_ld["g"][q % 2], 16)
                sp.dma_start(raw_u[q % 2][:], ffn_w_up[0, :, f].rearrange("(k p) f -> p k f", p=P)).then_inc(f_ld["u"][q % 2], 16)

            dense_gu(0)
            for q in range(-1, STEPS):
                if q + 1 < STEPS and q >= 0:
                    dense_gu(q + 1)
                if q >= 0:
                    if q >= 2:
                        sp.wait_ge(s["f_dL"], 2 * (q - 1))
                    sp.dma_start(raw_d[q % 2][:], ffn_w_down[0, q * FC:(q + 1) * FC, :].rearrange("(k p) f -> p k f", p=P))\
                        .then_inc(f_ld["d"][q % 2], 16)
                load_mod_rows(step_rows(q))
            mixer_loads(1)

            mg, mu, md = moe_w_gate[0], moe_w_up[0], moe_w_down[0]
            sp.wait_ge(s["wL"], 2 * NU)
            sp.wait_ge(s["yT_L"], 8)

            def expert_pair(pair, it2):
                for par in range(2):
                    for st in range(STEPS + 1):
                        q = par * STEPS + st
                        if st < STEPS:
                            sp.wait_ge(s["m_guL"], it2 * (4 * STEPS) + (2 * q + 2))
                            f = slice(st * FC, (st + 1) * FC)
                            sp.dma_start(raw_g[q % 2][:], mg[pair * 2 + par, :, f].rearrange("(k p) f -> p k f", p=P))\
                                .then_inc(m_ld["g"][q % 2], 16)
                            sp.dma_start(raw_u[q % 2][:], mu[pair * 2 + par, :, f].rearrange("(k p) f -> p k f", p=P))\
                                .then_inc(m_ld["u"][q % 2], 16)
                        if st >= 1:
                            qd = q - 1
                            sp.wait_ge(s["m_dL"], it2 * (4 * STEPS) + (2 * qd + 2))
                            sp.dma_start(raw_d[qd % 2][:],
                                         md[pair * 2 + par, (st - 1) * FC:st * FC, :].rearrange("(k p) f -> p k f", p=P))\
                                .then_inc(m_ld["d"][qd % 2], 16)

            with sp.Fori(0, NE // 2) as pair:
                expert_pair(pair, pair)
            sp.wait_ge(s["npass"], 1)
            npass = sp.value_load(npass_i[0:1, 0:1], min_val=1, max_val=2)
            with sp.If(npass > 1):
                with sp.Fori(0, NE // 2) as pair:
                    expert_pair(pair, pair + NE // 2)
            it2 = npass * (NE // 2)
            sp.wait_ge(s["m_guL"], it2 * (4 * STEPS) + 2)
            sp.dma_start(raw_g[0][:], mg[0, :, 0:FC].rearrange("(k p) f -> p k f", p=P)).then_inc(m_ld["g"][0], 16)
            sp.dma_start(raw_u[0][:], mu[0, :, 0:FC].rearrange("(k p) f -> p k f", p=P)).then_inc(m_ld["u"][0], 16)
            for t in range(TT):
                sp.wait_ge(s["x_ln"], 7 + t)
                sp.dma_start(out[0, t * P:(t + 1) * P, :], x_sb[:, t, :]).then_inc(s["stored"], 16)
            sp.wait_ge(s["stored"], 16 * TT)

        @block.gpsimd
        def _(pool):
            n = [0]

            def link(ins):
                n[0] += 1
                ins.then_inc(s["pool_chain"], 1)
                pool.wait_ge(s["pool_chain"], n[0])

            link(pool.memset(stage[:], 0.0))
            pool.dma_start(stage[0:96, :], b_mod.rearrange("l (j p) -> (l j) p", p=P)).then_inc(s["stage_ld"], 16)
            pool.dma_start(stage[96:104, :], c.rearrange("a (j p) -> (a j) p", p=P)).then_inc(s["stage_ld"], 16)
            pool.dma_start(stage[104:108, :], b_a.rearrange("l (j p) -> (l j) p", p=P)).then_inc(s["stage_ld"], 16)
            pool.dma_start(wr[:], w_router[0].rearrange("(k p) e -> p k e", p=P)).then_inc(s["small_ld"], 16)
            pool.dma_start(br_row[:], b_router[0:1, :].broadcast_to([P, NE])).then_inc(s["small_ld"], 16)
            link(pool.memset(ident[:], 0.0))
            link(pool.affine_select(out=ident[:], in_=ident[:], compare_op=ALU.not_equal, fill=1.0, base=0,
                                    pattern=[[-1, P]], channel_multiplier=1))
            link(pool.memset(ones[:], 1.0))
            pool.affine_select(out=upper[:], in_=ones[:, 0:P], compare_op=ALU.is_gt, fill=0.0, base=0,
                               pattern=[[1, P]], channel_multiplier=-1)
            pool.affine_select(out=upper_eq[:], in_=ones[:, 0:P], compare_op=ALU.is_ge, fill=0.0, base=0,
                               pattern=[[1, P]], channel_multiplier=-1)
            link(pool.iota(dist[:], pattern=[[1, T]], base=-P, channel_multiplier=-1, allow_small_or_imprecise_dtypes=True))
            link(pool.affine_select(out=dist[:], in_=dist[:], compare_op=ALU.is_ge, fill=NEG, base=P,
                                    pattern=[[-1, T]], channel_multiplier=1))
            link(pool.memset(ahead[:], 0.0))
            link(pool.affine_select(out=ahead[:], in_=ahead[:], compare_op=ALU.is_ge, fill=FILL, base=P,
                                    pattern=[[-1, T]], channel_multiplier=1))
            pool.iota(slot_id[:], pattern=[[1, P]], base=0, channel_multiplier=0, allow_small_or_imprecise_dtypes=True)
            pool.iota(rev8[:], pattern=[[-1, NE]], base=NE, channel_multiplier=0, allow_small_or_imprecise_dtypes=True)
            pool.memset(half_neg[:], -0.5).then_inc(s["const"], 1)

            def load_rows(ph):
                l, k = ph // 2, ph % 2
                pool.dma_start(lng_row[:], ln_g[l, k:k + 1, :].broadcast_to([P, D])).then_inc(s["rows_ld"], 16)
                pool.dma_start(lnb_row[:], ln_b[l, k:k + 1, :].broadcast_to([P, D])).then_inc(s["rows_ld"], 16)

            def norm_power(ph):
                for t in range(TT):
                    pool.wait_ge(s["mv"], ph * TT + t + 1)
                    link(pool.tensor_scalar(veps[:, t:t + 1], mv[:, t, 1:2], EPS, None, ALU.add))
                    pool.tensor_tensor(rstd[:, t:t + 1], veps[:, t:t + 1], half_neg[:, 0:1], ALU.pow)\
                        .then_inc(s["rstd"], 1)

            for l in range(DEPTH):
                if l:
                    pool.wait_ge(s["x_ln"], 4 * l)
                else:
                    pool.wait_ge(s["mod_sum"], 1)
                load_rows(2 * l)
                pool.dma_start(gnorm[:], gla_norm_g[l:l + 1, :].broadcast_to([P, B_DV])).then_inc(s["wa2_ld"], 16)
                link(pool.memset(wa2[:], 0.0))
                pool.dma_start(wa2[0:RANK, :], w_a2[l]).then_inc(s["wa2_ld"], 16)
                for part in (akP, ikP, qfP, qxP):
                    pool.memset(part[:], 0.0)
                pool.memset(baT[:], 0.0).then_inc(s["pads"], 1)
                for t in range(TT):
                    pool.wait_ge(s["ssq"], l * TT + t + 1)
                    link(pool.tensor_scalar(rms[:, t, :], ssq[:, t, :], 1.0 / B_DV, EPS, ALU.mult, ALU.add))
                    pool.tensor_tensor(rms[:, t, :], rms[:, t, :], half_neg[:, 4:8], ALU.pow).then_inc(s["rms"], 1)
                norm_power(2 * l)
                pool.wait_ge(s["x_ln"], 4 * l + 2)
                if l == 0:
                    load_rows(1)
                    norm_power(1)
            pool.memset(yH.bitcast(F32), 0.0)
            pool.memset(yL.bitcast(F32), 0.0)
            pool.memset(one_S[:].bitcast(F32), 0.0).then_inc(s["zeros"], 1)
            pool.wait_ge(s["m_end"], 1)
            load_rows(3)
            norm_power(3)

        def moe_act_down(act, q, it2):
            act.wait_ge(m_ld["d"][q % 2], it2 * (16 * STEPS) + 16 * (q // 2 + 1))
            for j in range(2):
                act.wait_ge(s["m_d"], it2 * (4 * STEPS) + (2 * q + j + 1))
                nc.scalar.activation(d_H[:, j, :], raw_d[q % 2][:, j, :], ACT.Copy).then_inc(s["m_dH"], 1)
            act.wait_ge(s["m_t"], it2 * (2 * STEPS) + (q + 2))
            act.wait_ge(s["m_d"], it2 * (4 * STEPS) + (2 * q + 2))
            nc.scalar.activation(hidT_H[:, 0], bank[4][:, 0:256].rearrange("p (a t) -> p a t", a=2), ACT.Copy).then_inc(s["m_tH"], 1)

        @block.scalar
        def _(act):
            A = nc.scalar.activation
            n = [0]

            def link(ins):
                n[0] += 1
                ins.then_inc(s["act_chain"], 1)
                act.wait_ge(s["act_chain"], n[0])

            act.wait_ge(s["cols_rd"], 1)
            A(c_act[:], cols[:, 96:104], ACT.Silu).then_inc(s["cact"], 1)

            def conv_unit(l, u):
                act.wait_ge(w_ld[u % 2], 16 * (l * (9 if u % 2 == 0 else 8) + u // 2 + 1))
                if u >= 2:
                    act.wait_ge(s["proj"], l * NU + u - 1)
                elif l:
                    act.wait_ge(s["f_gu"], 2 * STEPS)
                dst, src = gu_H0[:, :, (u % 2) * 256:(u % 2) * 256 + 256], wraw[u % 2]
                if u in (U_IKW, U_AKV):
                    w = W_IN_UNITS[u][1] - 64
                    A(dst[:, :, 0:128].rearrange("p k (r c) -> p k r c", r=2),
                      src[:, :, 0:64].unsqueeze(2).broadcast_to([P, KT, 2, 64]), ACT.Copy)
                    A(dst[:, :, 128:128 + w], src[:, :, 64:64 + w], ACT.Copy).then_inc(s["wH"], 1)
                else:
                    w = unit_src(l, u)[1]
                    A(dst[:, :, 0:w], src[:, :, 0:w], ACT.Copy).then_inc(s["wH"], 1)

            def evacuate(l, u):
                b = bank[4 + u % 4]
                act.wait_ge(s["proj"], l * NU + u + 1)
                two = b[:].rearrange("p (a t) -> p a t", a=2)
                if u in (U_IQ0, U_IQ1):
                    last = A(iqT[:, 2 * u:2 * u + 2, :], two, ACT.Copy, scale=SQ)
                elif u in (U_AQ0, U_AQ1):
                    v = u - U_AQ0
                    last = A(aqT[:, 2 * v:2 * v + 2, :], two, ACT.Copy, scale=SQ)
                elif u in (U_IKW, U_AKV):
                    act.wait_ge(s["pads"], l + 1)
                    dst = ikP if u == U_IKW else akP
                    A(dst[0:64, 0, :], b[0:64, 0:T], ACT.Copy)
                    last = A(dst[64:128, 1, :], b[64:128, 0:T], ACT.Copy)
                    if u == U_IKW:
                        last = A(iw[:], b[:, T:T + 16].rearrange("p (t h) -> p t h", t=2), ACT.Copy, scale=8 ** -0.5)
                    else:
                        last = A(av[:], b[:, T:T + 128].rearrange("p (t h) -> p t h", t=2), ACT.Copy)
                elif u == U_BQ:
                    last = A(bqT[:], two, ACT.Copy, scale=SQ)
                elif u == U_BK:
                    last = A(bkT[:], two, ACT.Copy)
                elif u == U_BA:
                    last = A(baT[0:RANK, :], b[0:RANK, 0:T], ACT.Copy)
                elif u in (U_BV0, U_BV1):
                    v = u - U_BV0
                    last = A(bv[:, :, v * 256:v * 256 + 256], two, ACT.Copy)
                else:
                    v = u - U_BG0
                    last = A(sbg[:, :, v * 256:v * 256 + 256], two, ACT.Silu)
                last.then_inc(s["evac"], 1)

            def high_of_tokens(ph):
                for h in range(2):
                    act.wait_ge(s["hfull"], ph * KT + 4 * h + 4)
                    A(hT_H[:, 4 * h:4 * h + 4, :], hfull[:, 4 * h:4 * h + 4, :], ACT.Copy).then_inc(s["hT_H"], 1)

            def gate_row(ph, base=4):
                for h in range(2):
                    act.wait_ge(s["g_ps"], 2 * ph + h + 1)
                    A(g_row[:, h * 512:h * 512 + 512], bank[base + h][:], ACT.Copy).then_inc(s["g_row"], 1)

            def mixer(l):
                conv_unit(l, 0)
                conv_unit(l, 1)
                high_of_tokens(2 * l)
                for u in range(NIN):
                    evacuate(l, u)
                    conv_unit(l, u + 2)
                    if u == U_IKW:
                        for k in range(NG):
                            act.wait_ge(s["idx_ps"], l * NG + k + 1)
                            if k >= 2:
                                act.wait_ge(s["idxacc"], l * NG + k - 1)
                            A(relu[k % 2][:], bank[k % 4][:], ACT.Relu).then_inc(s["relu"], 1)
                    if u == U_BV0:
                        act.wait_ge(s["z_ps"], l + 1)
                        for pr in range(2):
                            last = A(dec0[:, pr, :], bank[0][:, pr * T:(pr + 1) * T], ACT.Abs,
                                     bias=cols[:, 104 + 2 * l + pr:105 + 2 * l + pr])
                        link(last)
                        link(A(dec0[:], dec0[:], ACT.Exp, scale=-1.0))
                        A(dec0[:], dec0[:], ACT.Ln, bias=1.0).then_inc(s["az"], 1)
                act.wait_ge(s["decay"], l + 1)
                A(dec0[:], dec0[:], ACT.Exp).then_inc(s["qe"], 1)
                for pr in range(2):
                    A(kx[:, pr, :], bT[:, pr, 0:P], ACT.Exp, scale=-1.0, bias=bT[:, pr, P - 1:P])
                    A(dec1[:, pr, 0:P], bT[:, pr, P:T], ACT.Exp, bias=nb127[:, pr:pr + 1]).then_inc(s["kx_e"], 1)
                for pr in range(2):
                    act.wait_ge(s["kfac_rd"], 2 * l + pr + 1)
                    A(kfac[:, pr], kfac[:, pr], ACT.Exp).then_inc(s["ke"], 1)
                act.wait_ge(s["at_ps"], 3 * l + 3)
                A(at_sb[:, 2, :], bank[2][:], ACT.Copy).then_inc(s["at_sb"], 1)
                for t in range(TT):
                    act.wait_ge(s["o_ps"], l * TT + t + 1)
                    ob = bank[3] if t == 0 else bank[0]
                    for h in range(B_HEADS):
                        last = A(relu[t][:, h * B_DV:(h + 1) * B_DV], ob[:, h * B_DV:(h + 1) * B_DV], ACT.Square,
                                 accum_out=ssq[:, t, h:h + 1])
                    last.then_inc(s["ssq"], 1)
                for t in range(TT):
                    act.wait_ge(s["nmax"], l * TT + t + 1)
                    for h in range(A_HEADS):
                        last = A(prob[t][:, h, :], prob[t][:, h, :], ACT.Exp, bias=nmax[:, t, h:h + 1],
                                 accum_out=rsum[:, t, h:h + 1])
                    last.then_inc(s["pexp"], 1)
                    for g in range(2) if t == 0 else range(2, NG):
                        act.wait_ge(s["pt_ps"], l * NG + g + 1)
                        dst = pT0[:, 4 * g:4 * g + 4, :] if t == 0 else pT1[:, 4 * (g - 2):4 * (g - 2) + 4, :]
                        A(dst, bank[1 + g % 2][:].rearrange("p (a b) -> p a b", a=4), ACT.Copy).then_inc(s["pt_sb"], 1)
                for b in range(4):
                    act.wait_ge(s["yT_ps"], 4 * l + b + 1)
                    A(hT_H[:, 2 * b:2 * b + 2, :], bank[b][:].rearrange("p (a t) -> p a t", a=2), ACT.Copy)\
                        .then_inc(s["yT_H"], 1)
                for u in range(NIN + 2, NU):
                    conv_unit(l, u)
                    if u == NIN + 2:
                        gate_row(2 * l, 0)

            mixer(0)

            def dense_conv_gu(q):
                if q == 0:
                    act.wait_ge(s["proj"], NU)
                elif q == 1:
                    act.wait_ge(s["yT_L"], 4)
                else:
                    act.wait_ge(s["f_gu"], 2 * (q - 1))
                for i, (k, raw) in enumerate((("g", raw_g), ("u", raw_u))):
                    act.wait_ge(f_ld[k][q % 2], 16 * (q // 2 + 1))
                    A(gu_H[q % 2][:, :, i * FC:(i + 1) * FC], raw[q % 2][:], ACT.Copy).then_inc(s["f_guH"], 1)

            dense_conv_gu(0)
            gate_row(1)
            high_of_tokens(1)
            for q in range(STEPS + 1):
                if q + 1 < STEPS:
                    dense_conv_gu(q + 1)
                if q < STEPS:
                    act.wait_ge(s["f_gu"], 2 * q + 1)
                    if q >= 1:
                        act.wait_ge(s["f_hid"], 2 * q - 1)
                    A(silu_g[:, 0, :], bank[0][:, 0:FC], ACT.Silu).then_inc(s["f_silu"], 1)
                if q >= 1:
                    act.wait_ge(f_ld["d"][(q - 1) % 2], 16 * ((q - 1) // 2 + 1))
                    for j in range(2):
                        if q >= 2:
                            act.wait_ge(s["f_d"], 4 * (q - 1))
                        A(d_H[:, j, :], raw_d[(q - 1) % 2][:, j, :], ACT.Copy).then_inc(s["f_dH"], 1)
                    act.wait_ge(s["f_t"], 2 * (q - 1) + 2)
                    if q >= 2:
                        act.wait_ge(s["f_d"], 4 * (q - 1))
                    A(hidT_H[:, 1], bank[7][:, 0:256].rearrange("p (a t) -> p a t", a=2), ACT.Copy).then_inc(s["f_tH"], 1)
                if q < STEPS:
                    act.wait_ge(s["f_gu"], 2 * q + 2)
                    if q >= 1:
                        act.wait_ge(s["f_hid"], 2 * q)
                    A(silu_g[:, 1, :], bank[1][:, 0:FC], ACT.Silu).then_inc(s["f_silu"], 1)
                    act.wait_ge(s["f_t"], 2 * q + 1)
                    if q >= 1:
                        act.wait_ge(s["f_d"], 4 * (q - 1) + 2)
                    A(hidT_H[:, 0], bank[4][:, 0:256].rearrange("p (a t) -> p a t", a=2), ACT.Copy).then_inc(s["f_tH"], 1)

            mixer(1)

            def moe_conv_gu(q, it2):
                if q:
                    act.wait_ge(s["m_gu"], it2 * (2 * STEPS) + q)
                for i, (k, raw) in enumerate((("g", raw_g), ("u", raw_u))):
                    act.wait_ge(m_ld[k][q % 2], it2 * (16 * STEPS) + 16 * (q // 2 + 1))
                    A(gu_H[q % 2][:, :, i * FC:(i + 1) * FC], raw[q % 2][:], ACT.Copy).then_inc(s["m_guH"], 1)

            act.wait_ge(s["x_ln"], 6)
            act.wait_ge(s["proj"], 2 * NU)
            moe_conv_gu(0, 0)
            act.wait_ge(s["lg8"], 1)
            A(v2[:, 3, :], v2[:, 2, :], ACT.Exp).then_inc(s["expd"], 1)
            for t in range(TT):
                A(xH[t][:], x_sb[:, t, :], ACT.Copy).then_inc(s["xsplit"], 1)

            def gathered(E):
                for kt in range(KT):
                    act.wait_ge(s["xg_ps"], E * 2 + kt // 4 + 1)
                    A(xg_full[:, kt, :], bank[5 + kt // 4][:, (kt % 4) * P:(kt % 4 + 1) * P], ACT.Identity,
                      scale=modT[:, 48 + 32 + kt:48 + 33 + kt], bias=modT[:, 48 + 24 + kt:48 + 25 + kt])\
                        .then_inc(s["xg_full"], 1)

            gathered(0)
            act.wait_ge(s["xg_full"], KT)
            A(xgH, xg_full[:], ACT.Copy).then_inc(s["xg_H"], 1)
            act.wait_ge(s["npass"], 1)
            npass = act.value_load(npass_i[0:1, 0:1], min_val=1, max_val=2)
            with act.Fori(0, npass) as ps:
                with act.Fori(0, NE // 2) as pair:
                    it2 = ps * (NE // 2) + pair
                    for par in range(2):
                        for st in range(STEPS):
                            q = par * STEPS + st
                            Q = lambda m, a: it2 * (2 * STEPS * m) + (m * q + a)
                            moe_conv_gu(q + 1, it2)
                            act.wait_ge(s["m_gu"], Q(1, 2))
                            act.wait_ge(s["m_hid"], Q(1, 2))
                            A(silu_g[:, 0, :], bank[q % 2][:, 0:FC], ACT.Silu).then_inc(s["m_silu"], 1)
                            if st >= 1:
                                moe_act_down(act, q - 1, it2)
                        E = it2 * 2 + par
                        for kt in range(KT):
                            act.wait_ge(s["xg_ps"], E * 2 + (2 + kt // 4 + 1))
                            if kt == 0:
                                act.wait_ge(s["xg_L"], E + 1)
                            A(xg_full[:, kt, :], bank[5 + kt // 4][:, (kt % 4) * P:(kt % 4 + 1) * P], ACT.Identity,
                              scale=modT[:, 48 + 32 + kt:48 + 33 + kt], bias=modT[:, 48 + 24 + kt:48 + 25 + kt])\
                                .then_inc(s["xg_full"], 1)
                        moe_act_down(act, par * STEPS + STEPS - 1, it2)
                        act.wait_ge(s["xg_full"], E * KT + 2 * KT)
                        act.wait_ge(s["m_gu"], it2 * (2 * STEPS) + ((par + 1) * STEPS + 1))
                        A(xgH, xg_full[:], ACT.Copy).then_inc(s["xg_H"], 1)
                        act.wait_ge(s["m_d"], it2 * (4 * STEPS) + (2 * STEPS * (par + 1) + 2))
                        act.wait_ge(s["m_sc"], E * 4 + 4)
                        for h in range(2):
                            A(yH[:, h * 512:h * 512 + 512], bank[2 + h][:], ACT.Copy)\
                                .then_inc(s["m_yH"], 1)
            act.wait_ge(s["m_end"], 1)
            gate_row(3)


        @block.tensor
        def _(pe):
            mm = nc.tensor.matmul

            def transposed_tokens(src, signal):
                for b in range(4):
                    for i in range(2):
                        for t in range(TT):
                            kt = 2 * b + i
                            last = nc.tensor.transpose(bank[b][:, i * T + t * P:i * T + (t + 1) * P],
                                                       src[:, t, kt * P:(kt + 1) * P], ident[:])
                    last.then_inc(s[signal], 1)

            def gate_row(ph, diag, base=4):
                pe.wait_ge(s["gdiag"], ph + 1)
                for h in range(2):
                    mm(bank[base + h][:], ones[:, 0:P], diag[:, h * 512:(h + 1) * 512], start=True, stop=True)\
                        .then_inc(s["g_ps"], 1)

            pe.wait_ge(s["const"], 1)
            pe.wait_ge(s["stage_ld"], 48)
            nc.tensor.transpose(bank[7][:, 0:P], stage[:], ident[:]).then_inc(s["stageT"], 1)
            pe.wait_ge(s["cact"], 1)
            pe.wait_ge(s["x_ld"], 32)
            transposed_tokens(x_sb, "xT_ps")

            def sum_chunk(acc, o):
                for k in range(KT):
                    last = mm(o[:, k:k + 1], acc[:, k * P:(k + 1) * P], ones[:, 0:1], start=True, stop=True)
                return last
            pe.wait_ge(s["mod_sum"], 1)
            sum_chunk(ycat[:, 0, :], bank[6][:, 0:KT])
            sum_chunk(ycat[:, 1, :], bank[6][:, KT:2 * KT]).then_inc(s["mod_ps"], 1)

            def project(l, u):
                pe.wait_ge(s["wL"], l * NU + u + 1)
                if u == 0:
                    pe.wait_ge(s["hT_L"], 4 * l + 2)
                    if l:
                        pe.wait_ge(s["modT"], 11)
                elif 4 <= u < NIN:
                    pe.wait_ge(s["evac"], l * NIN + u - 3)
                    if l == 0 and u == U_BA + 4:
                        pe.wait_ge(s["modT"], 3)
                elif u == NIN:
                    pe.wait_ge(s["yT_L"], 4 * (l + 1))
                elif u == NIN + 1 and l == 0:
                    pe.wait_ge(s["modT"], 5)
                b = bank[4 + (u % 4 if u < NIN else u - NIN)]
                base = (u % 2) * 256
                if l == 0 and u == U_BA:
                    for a in (2, 3):
                        pe.wait_ge(s["row_rd"], (a - 1) * KT)
                        sum_chunk(mod_acc[a % 2], b[:, T + a * KT:T + (a + 1) * KT]).then_inc(s["mod_ps"], 1)
                WH, WL = gu_H0[:, :, base:base + 256], gu_L0[:, :, base:base + 256]
                if u in (U_BV0, U_BV1, U_BG0, U_BG1) or u >= NIN:
                    for t in range(TT):
                        tok = slice(t * P, (t + 1) * P)
                        for kt in range(KT):
                            last = mm3(b[:, t * 256:(t + 1) * 256], hT_H[:, kt, tok], hT_L[:, kt, tok],
                                       WH[:, kt, :], WL[:, kt, :], kt == 0, kt == KT - 1)
                else:
                    for ct in range(2 if W_IN_UNITS[u][1] == 256 else 1):
                        cc = slice(ct * P, (ct + 1) * P)
                        for kt in range(KT):
                            last = mm3(b[:, ct * T:(ct + 1) * T], WH[:, kt, cc], WL[:, kt, cc],
                                       hT_H[:, kt, :], hT_L[:, kt, :], kt == 0, kt == KT - 1)
                    if u in (U_IKW, U_AKV):
                        w = W_IN_UNITS[u][1] - 64
                        for t in range(TT):
                            tok = slice(t * P, (t + 1) * P)
                            for kt in range(KT):
                                last = mm3(b[:, T + t * w:T + (t + 1) * w], hT_H[:, kt, tok], hT_L[:, kt, tok],
                                           WH[:, kt, P:P + w], WL[:, kt, P:P + w], kt == 0, kt == KT - 1)
                last.then_inc(s["proj"], 1)

            def head_products(l, lhsT, rhs, banks, free, signal):
                for k, (t, heads, keys) in enumerate(HEAD_GROUPS):
                    if k >= 4:
                        pe.wait_ge(s[free], l * NG + k - 3)
                    for i, h in enumerate(heads):
                        last = mm(bank[banks + k % 4][:, i * keys:(i + 1) * keys], lhsT[:, h // 2, t * P:(t + 1) * P],
                                  rhs[:, h % 2, 0:keys], start=True, stop=True)
                    last.then_inc(s[signal], 1)

            def mixer(l):
                if l:
                    pe.wait_ge(s["x_ln"], 4 * l)
                    transposed_tokens(x_sb, "xT_ps")
                for u in range(NIN):
                    project(l, u)
                    if u == U_AQ0:
                        pe.wait_ge(s["evac"], l * NIN + 3)
                        head_products(l, iqT, ikP, 0, "relu", "idx_ps")
                    if u == U_BV0:
                        pe.wait_ge(s["evac"], l * NIN + 9)
                        pe.wait_ge(s["wa2_ld"], 32 * (l + 1))
                        pe.wait_ge(s["relu"], NG * (l + 1))
                        for pr in range(2):
                            last = mm(bank[0][:, pr * T:(pr + 1) * T], wa2[:, pr * P:(pr + 1) * P], baT[:],
                                      start=True, stop=True)
                        last.then_inc(s["z_ps"], 1)
                pe.wait_ge(s["gla_in"], l + 1)
                for tb in range(2):
                    o = bank[tb][:].rearrange("p (h t) -> p h t", h=4)
                    for pr in range(2):
                        for j in range(NBLK):
                            q0 = j * BLK
                            last = mm(o[:, 2 * pr:2 * pr + 2, q0:q0 + BLK], kfac[:, pr, tb, j, :],
                                      qfP[:, pr, :, tb * P + q0:tb * P + q0 + BLK], start=True, stop=True)
                    last.then_inc(s["at_ps"], 1)
                for pr in range(2):
                    last = mm(bank[2][:, pr * T:(pr + 1) * T], kx[:, pr, :], qxP[:, pr, :, :].rearrange("p a b -> p (a b)"),
                              start=True, stop=True)
                last.then_inc(s["at_ps"], 1)
                pe.wait_ge(s["evac"], NIN * (l + 1))
                head_products(l, aqT, akP, 4, "lg_sb", "lg_ps")
                pe.wait_ge(s["at_msk"], 2 * l + 1)
                for h in range(B_HEADS):
                    e = slice(h * B_DV, (h + 1) * B_DV)
                    last = mm(bank[3][:, e], at_sb[:, 0, e], bv[:, 0, e], start=True, stop=True)
                last.then_inc(s["o_ps"], 1)
                pe.wait_ge(s["at_msk"], 2 * l + 2)
                pe.wait_ge(s["at_sb"], l + 1)
                for h in range(B_HEADS):
                    e = slice(h * B_DV, (h + 1) * B_DV)
                    mm(bank[0][:, e], at_sb[:, 1, e], bv[:, 1, e], start=True, stop=False)
                    last = mm(bank[0][:, e], at_sb[:, 2, e], bv[:, 0, e], start=False, stop=True)
                last.then_inc(s["o_ps"], 1)
                for t in range(TT):
                    pe.wait_ge(s["pexp"], TT * l + t + 1)
                    for g in range(2) if t == 0 else range(2, NG):
                        if g >= 2:
                            pe.wait_ge(s["pt_sb"], l * NG + g - 1)
                        for i in range(4):
                            if t == 0:
                                src = prob0[:, 4 * g + i, :]
                            else:
                                n = 4 * (g - 2) + i
                                src = prob1[:, n // 2, (n % 2) * P:(n % 2 + 1) * P]
                            last = nc.tensor.transpose(bank[1 + g % 2][:, i * P:(i + 1) * P], src, ident[:])
                        last.then_inc(s["pt_ps"], 1)
                    pe.wait_ge(s["pt_sb"], l * NG + (2 if t == 0 else NG))
                    pe.wait_ge(s["lg_sb"], l * NG + 3 + t)
                    for h in range(A_HEADS):
                        e = slice(h * 64, (h + 1) * 64)
                        if t == 0:
                            last = mm(bank[6][:, e], pT0[:, h, :], av[:, 0, :], start=True, stop=True)
                        else:
                            mm(bank[7][:, e], pT1[:, 2 * h, :], av[:, 0, :], start=True, stop=False)
                            last = mm(bank[7][:, e], pT1[:, 2 * h + 1, :], av[:, 1, :], start=False, stop=True)
                    last.then_inc(s["pv_ps"], 1)
                if l == 0:
                    pe.wait_ge(s["lg_sb"], NG)
                    for a in (4, 5):
                        pe.wait_ge(s["row_rd"], (a - 1) * KT)
                        sum_chunk(mod_acc[a % 2], bank[5][:, a * KT:(a + 1) * KT]).then_inc(s["mod_ps"], 1)
                pe.wait_ge(s["ycat"], l + 1)
                transposed_tokens(ycat, "yT_ps")
                for u in range(NIN, NU):
                    project(l, u)
                    if u == NIN:
                        gate_row(2 * l, prob0[:].rearrange("p h t -> p (h t)"), 0)

            def gate_up(b, sH, sL, buf):
                for kt in range(KT):
                    last = mm3(b[:], sH(kt), sL(kt), gu_H[buf][:, kt, :], gu_L[buf][:, kt, :], kt == 0, kt == KT - 1)
                return last

            def hidden_transposes(t, b):
                for j in range(2):
                    last = nc.tensor.transpose(b[:, j * P:(j + 1) * P], hid[:, t, j * P:(j + 1) * P], ident[:])
                return last

            def down(t, j, y, first, last_of_all):
                for h in range(2):
                    cc = slice(h * 512, (h + 1) * 512)
                    last = mm3(y[h][:], hidT_H[:, t, j, :], hidT_L[:, t, j, :], d_H[:, j, cc], d_L[:, j, cc],
                               first, last_of_all)
                return last

            mixer(0)

            pe.wait_ge(s["x_ln"], 2)
            transposed_tokens(x_sb, "xT_ps")
            gate_row(1, ycat[:, 0, :])
            pe.wait_ge(s["hT_L"], 4)
            pe.wait_ge(s["g_row"], 4)
            ybank = [[bank[2], bank[3]], [bank[5], bank[6]]]
            for q in range(STEPS + 1):
                p = q - 1
                if q < STEPS:
                    pe.wait_ge(s["f_guL"], 2 * (q + 1))
                    if q >= 1:
                        pe.wait_ge(s["f_hid"], 2 * p + 1)
                    gate_up(bank[0], lambda k: hT_H[:, k, 0:P], lambda k: hT_L[:, k, 0:P], q % 2).then_inc(s["f_gu"], 1)
                if q >= 1:
                    pe.wait_ge(s["f_hid"], 2 * p + 2)
                    if q >= 2:
                        pe.wait_ge(s["f_tL"], 2 * p)
                    hidden_transposes(1, bank[7]).then_inc(s["f_t"], 1)
                if q < STEPS:
                    gate_up(bank[1], lambda k: hT_H[:, k, P:T], lambda k: hT_L[:, k, P:T], q % 2).then_inc(s["f_gu"], 1)
                if q >= 1:
                    for t in range(2):
                        pe.wait_ge(s["f_tL"], 2 * p + 1 + t)
                        for j in range(2):
                            pe.wait_ge(s["f_dL"], 2 * p + j + 1)
                            down(t, j, ybank[t], p == 0 and j == 0, p == STEPS - 1 and j == 1).then_inc(s["f_d"], 1)
                if q < STEPS:
                    pe.wait_ge(s["f_hid"], 2 * q + 1)
                    if q in MOD_AT_STEP:
                        a = MOD_AT_STEP[q]
                        pe.wait_ge(s["row_rd"], ROWS_L0 + (a + 1) * KT)
                        pe.wait_ge(s["f_tL"], 2 * q)
                        sum_chunk(mod_acc[a % 2], bank[4][:, T:T + KT]).then_inc(s["mod_ps"], 1)
                    hidden_transposes(0, bank[4]).then_inc(s["f_t"], 1)
            pe.wait_ge(s["row_rd"], len(MOD_ROWS))
            sum_chunk(mod_acc[1], bank[4][:, T:T + KT]).then_inc(s["mod_ps"], 1)

            mixer(1)

            pe.wait_ge(s["x_ln"], 6)
            transposed_tokens(x_sb, "xT_ps")
            pe.wait_ge(s["hfull"], 4 * KT)
            pe.wait_ge(s["small_ld"], 32)
            for t in range(TT):
                for kt in range(KT):
                    last = mm(bank[7][:, t * NE:(t + 1) * NE], hfull[:, kt, t * P:(t + 1) * P], wr[:, kt, :],
                              start=(kt == 0), stop=(kt == KT - 1))
            last.then_inc(s["rt_ps"], 1)
            pe.wait_ge(s["sel"], 1)
            sel = rt[8]
            mm(bank[7][:, 16:24], upper[:], sel[:, 0, :], start=True, stop=True).then_inc(s["m_d"], 2)
            mm(bank[7][:, 24:32], ones[:, 0:P], sel[:, 0, :], start=True, stop=False).then_inc(s["m_gu"], 1)
            mm(bank[7][:, 24:32], upper[:], sel[:, 1, :], start=False, stop=True).then_inc(s["m_t"], 1)
            mm(bank[7][:, 32:40], ones[:, 0:P], sel[:, 0, :], start=True, stop=False)
            mm(bank[7][:, 32:40], ones[:, 0:P], sel[:, 1, :], start=False, stop=True).then_inc(s["rank_ps"], 1)

            def gather():
                for b in range(2):
                    for i in range(4):
                        kt = 4 * b + i
                        for t in range(TT):
                            for part in (xH, xL):
                                last = mm(bank[5 + b][:, i * P:(i + 1) * P], part[t][:, kt * P:(kt + 1) * P],
                                          one_G[:, t, :], start=(t == 0 and part is xH), stop=(t == 1 and part is xL))
                    last.then_inc(s["xg_ps"], 1)

            def scatter():
                for i, b in enumerate((5, 6, 7, 2)):
                    t, h = i // 2, i % 2
                    tok, cc = slice(t * P, (t + 1) * P), slice(h * 512, (h + 1) * 512)
                    mm(bank[b][:], one_S[:, tok], yH[:, cc], start=True, stop=False)
                    mm(bank[b][:], one_S[:, tok], yL[:, cc], start=False, stop=True).then_inc(s["m_sc"], 1)

            pe.wait_ge(s["G"], 2)
            pe.wait_ge(s["xsplit"], 2)
            pe.wait_ge(s["xsplitL"], 2)
            gather()
            pe.wait_ge(s["zeros"], 1)
            npass = pe.value_load(npass_i[0:1, 0:1], min_val=1, max_val=2)
            with pe.Fori(0, npass) as ps:
                with pe.Fori(0, NE // 2) as pair:
                    it2 = ps * (NE // 2) + pair

                    def moe_down(q, st):
                        pe.wait_ge(s["m_tL"], it2 * (2 * STEPS) + (q + 2))
                        for j in range(2):
                            pe.wait_ge(s["m_dL"], it2 * (4 * STEPS) + (2 * q + j + 5))
                            down(0, j, [bank[2], bank[3]], st == 0 and j == 0, st == STEPS - 1 and j == 1)\
                                .then_inc(s["m_d"], 1)

                    def moe_transposes(q):
                        pe.wait_ge(s["m_hid"], it2 * (2 * STEPS) + (q + 3))
                        pe.wait_ge(s["m_tL"], it2 * (2 * STEPS) + (q + 1))
                        hidden_transposes(0, bank[4]).then_inc(s["m_t"], 1)

                    for par in range(2):
                        E = it2 * 2 + par
                        for st in range(STEPS):
                            q = par * STEPS + st
                            if st == 0:
                                pe.wait_ge(s["xg_L"], E + 1)
                            pe.wait_ge(s["m_guL"], it2 * (4 * STEPS) + (2 * q + 6))
                            pe.wait_ge(s["m_hid"], it2 * (2 * STEPS) + (q + 1))
                            gate_up(bank[q % 2], lambda k: xgH[:, k, :], lambda k: xgL[:, k, :], q % 2)\
                                .then_inc(s["m_gu"], 1)
                            if st == 0:
                                pe.wait_ge(s["m_yL"], E * 2 + 2)
                                pe.wait_ge(s["m_S"], E + 1)
                                scatter()
                            if st == 1:
                                moe_transposes(q - 1)
                                pe.wait_ge(s["m_acc"], E * 4 + 8)
                                for t in range(TT):
                                    last = nc.tensor.transpose(bank[7][:, t * P:(t + 1) * P],
                                                               one_G[:, t, :].bitcast(F32), ident[:])
                                last.then_inc(s["m_st"], 1)
                            if st >= 2:
                                moe_down(q - 2, st - 2)
                                moe_transposes(q - 1)
                        q = par * STEPS + STEPS - 1
                        pe.wait_ge(s["G"], E * 2 + 4)
                        gather()
                        moe_down(q - 1, STEPS - 2)
                        moe_transposes(q)
                        moe_down(q, STEPS - 1)
            n_done = npass * NE
            pe.wait_ge(s["m_yL"], n_done * 2 + 2)
            pe.wait_ge(s["m_S"], n_done + 1)
            pe.wait_ge(s["xg_full"], n_done * KT + KT)
            scatter()
            gate_row(3, xg_full[:].rearrange("p k t -> p (k t)"))

        @block.vector
        def _(dve):
            V = nc.vector
            n = [0]

            def link(ins):
                n[0] += 1
                ins.then_inc(s["dve_chain"], 1)
                dve.wait_ge(s["dve_chain"], n[0])

            dve.wait_ge(s["stageT"], 1)
            V.tensor_copy(cols[:], bank[7][:, 0:P]).then_inc(s["cols_rd"], 1)
            dve.wait_ge(s["cols_rd"], 1)

            def conditioning(l, a, o):
                c0 = 48 * l + 8 * a
                return V.scalar_tensor_tensor(out=modT[:, c0:c0 + 8], in0=o, scalar=0.0 if a % 3 == 0 else 1.0,
                                              in1=cols[:, c0:c0 + 8], op0=ALU.add, op1=ALU.add)

            dve.wait_ge(s["cact"], 1)
            for k in range(KT):
                dve.wait_ge(mod_ld[k], 16)
                for a in range(2):
                    w, acc = mod_first[:, k, a * D:(a + 1) * D], ycat[:, a, :]
                    if k == 0:
                        last = V.tensor_scalar(acc, w, c_act[:, 0:1], None, ALU.mult)
                    else:
                        last = V.scalar_tensor_tensor(out=acc, in0=w, scalar=c_act[:, k:k + 1], in1=acc,
                                                      op0=ALU.mult, op1=ALU.add)
                if k < KT - 1:
                    link(last)
            last.then_inc(s["mod_sum"], 1)
            dve.wait_ge(s["mod_ps"], 1)
            for a in range(2):
                last = conditioning(0, a, bank[6][:, a * KT:(a + 1) * KT])
            last.then_inc(s["modT"], 1)
            dve.wait_ge(s["modT"], 1)

            def gate_diag(ph, diag):
                g = modT[:, 48 * (ph // 2) + 16 + 24 * (ph % 2):48 * (ph // 2) + 24 + 24 * (ph % 2)]
                V.tensor_tensor(diag.rearrange("p (k t) -> p k t", k=KT), ident[:].unsqueeze(1).broadcast_to([P, KT, P]),
                                g.unsqueeze(2).broadcast_to([P, KT, P]), ALU.mult).then_inc(s["gdiag"], 1)

            def modulate(ph):
                base = 48 * (ph // 2) + 24 * (ph % 2)
                for kt in range(KT):
                    dve.wait_ge(s["xT_ps"], 4 * ph + kt // 2 + 1)
                    V.tensor_scalar(hfull[:, kt, :], bank[kt // 2][:, (kt % 2) * T:(kt % 2 + 1) * T],
                                    modT[:, base + 8 + kt:base + 9 + kt], modT[:, base + kt:base + kt + 1],
                                    ALU.mult, ALU.add).then_inc(s["hfull"], 1)

            def low_of_tokens(ph):
                for h in range(2):
                    k = slice(4 * h, 4 * h + 4)
                    dve.wait_ge(s["hT_H"], 2 * ph + h + 1)
                    V.tensor_tensor(hT_L[:, k, :], hfull[:, k, :], hT_H[:, k, :].bitcast(F32), ALU.subtract)\
                        .then_inc(s["hT_L"], 1)

            def condition_rows(rows):
                for n in rows:
                    l, a, k = MOD_ROWS[n]
                    row, acc = mod_ring[l][n % 4], mod_acc[a % 2][:]
                    dve.wait_ge(row_ld[n % 4], 16 * (n // 4 + 1))
                    if n:
                        dve.wait_ge(s["row_rd"], n)
                    if k == 0:
                        if l or a >= 4:
                            dve.wait_ge(s["mod_ps"], 4 + a if l else a - 2)
                        last = V.tensor_scalar(acc, row[:], c_act[:, 0:1], None, ALU.mult)
                    else:
                        last = V.scalar_tensor_tensor(out=acc, in0=row[:], scalar=c_act[:, k:k + 1], in1=acc,
                                                      op0=ALU.mult, op1=ALU.add)
                    last.then_inc(s["row_rd"], 1)

            def low_unit(l, u):
                dve.wait_ge(s["wH"], l * NU + u + 1)
                o = (u % 2) * 256
                H, L, src = gu_H0[:, :, o:o + 256], gu_L0[:, :, o:o + 256], wraw[u % 2]
                if u in (U_IKW, U_AKV):
                    w = W_IN_UNITS[u][1] - 64
                    V.tensor_tensor(L[:, :, 0:64], src[:, :, 0:64], H[:, :, 0:64].bitcast(F32), ALU.subtract)
                    V.tensor_tensor(L[:, :, 64:128], src[:, :, 0:64], H[:, :, 64:128].bitcast(F32), ALU.subtract)
                    V.tensor_tensor(L[:, :, 128:128 + w], src[:, :, 64:64 + w], H[:, :, 128:128 + w].bitcast(F32),
                                    ALU.subtract).then_inc(s["wL"], 1)
                else:
                    w = unit_src(l, u)[1]
                    V.tensor_tensor(L[:, :, 0:w], src[:, :, 0:w], H[:, :, 0:w].bitcast(F32), ALU.subtract)\
                        .then_inc(s["wL"], 1)

            def layer_norm(ph, terms):
                dve.wait_ge(s["g_row"], 2 * ph + 2)
                dve.wait_ge(s["rows_ld"], 32 * (ph + 1))
                for t in range(TT):
                    terms(t)
                    link(V.scalar_tensor_tensor(out=ycat[:, t, :], in0=x_sb[:, t, :], scalar=ALPHA, in1=ycat[:, t, :],
                                                op0=ALU.mult, op1=ALU.add))
                    for h in range(2):
                        last = V.bn_stats(stats[:, t, h, :], ycat[:, t, h * 512:(h + 1) * 512])
                    link(last)
                    V.bn_aggr(mv[:, t, :], stats[:, t]).then_inc(s["mv"], 1)
                for t in range(TT):
                    dve.wait_ge(s["rstd"], TT * ph + t + 1)
                    dve.wait_ge(s["mv"], TT * ph + t + 1)
                    link(V.tensor_scalar(ycat[:, t, :], ycat[:, t, :], mv[:, t, 0:1], rstd[:, t:t + 1],
                                         ALU.subtract, ALU.mult))
                    link(V.tensor_tensor(ycat[:, t, :], ycat[:, t, :], lng_row[:], ALU.mult))
                    V.tensor_tensor(x_sb[:, t, :], ycat[:, t, :], lnb_row[:], ALU.add).then_inc(s["x_ln"], 1)

            def indexer(l):
                for k, (t, heads, keys) in enumerate(HEAD_GROUPS):
                    dve.wait_ge(s["relu"], l * NG + k + 1)
                    for i, h in enumerate(heads):
                        src = relu[k % 2][:, i * keys:(i + 1) * keys]
                        if h == 0:
                            last = V.tensor_scalar(score[t][:], src, iw[:, t, h:h + 1], None, ALU.mult)
                        else:
                            last = V.scalar_tensor_tensor(out=score[t][:], in0=src, scalar=iw[:, t, h:h + 1],
                                                          in1=score[t][:], op0=ALU.mult, op1=ALU.add)
                        if i < len(heads) - 1:
                            link(last)
                    last.then_inc(s["idxacc"], 1)
                    dve.wait_ge(s["idxacc"], l * NG + k + 1)
                for t in range(TT):
                    last = V.tensor_tensor(score[t][:], score[t][:], ahead[:, P:T] if t == 0 else ahead[:], ALU.add)
                link(last)

            def select(t):
                for _ in range(TOPK // 8):
                    link(V.max(top8[:], score[t][:]))
                    link(V.match_replace(score[t][:], top8[:], score[t][:], -3.4e38))
                link(V.tensor_scalar(score[t][:], score[t][:], TAKEN, NEG, ALU.is_gt, ALU.mult))
                link(V.tensor_tensor(dsel[t][:], score[t][:], dist[:, P:T] if t == 0 else dist[:], ALU.add))

            def decay(l):
                dve.wait_ge(s["z_ps"], l + 1)
                dve.wait_ge(s["az"], l + 1)
                for pr in range(2):
                    last = V.tensor_scalar(dec1[:, pr, :], bank[0][:, pr * T:(pr + 1) * T],
                                           cols[:, 104 + 2 * l + pr:105 + 2 * l + pr], 0.0, ALU.add, ALU.min)
                link(last)
                link(V.tensor_tensor(dec1[:], dec1[:], dec0[:], ALU.subtract))
                link(V.tensor_scalar(dec1[:], dec1[:], 1.0 / 16.0, None, ALU.mult))
                for pr in range(2):
                    last = V.tensor_tensor_scan(bT[:, pr, :], ones[:], dec1[:, pr, :], 0.0, ALU.mult, ALU.add)
                link(last)
                V.tensor_scalar(nb127[:], bT[:, :, P - 1], -1.0, None, ALU.mult)
                blocks = bT[:].rearrange("p a (j b) -> p (a j) b", b=BLK)
                mid = blocks[:, :, BLK // 2:BLK // 2 + 1]
                V.tensor_tensor(dec0[:].rearrange("p a (j b) -> p (a j) b", b=BLK), blocks,
                                mid.broadcast_to([P, 2 * T // BLK, BLK]), ALU.subtract).then_inc(s["decay"], 1)
                for pr in range(2):
                    b = bT[:, pr, :].rearrange("p (a n) -> p a n", a=2)
                    r = bT[:, pr, :].rearrange("p (a j b) -> p a j b", a=2, b=BLK)[:, :, :, BLK // 2:BLK // 2 + 1]
                    link(V.tensor_tensor(kfac[:, pr], r.broadcast_to([P, 2, NBLK, P]),
                                         b.unsqueeze(2).broadcast_to([P, 2, NBLK, P]), ALU.subtract))
                    V.tensor_scalar(kfac[:, pr], kfac[:, pr], 40.0, None, ALU.min).then_inc(s["kfac_rd"], 1)

            def decay_products(l):
                dve.wait_ge(s["evac"], l * NIN + U_BK + 1)
                dve.wait_ge(s["pads"], l + 1)
                dve.wait_ge(s["qe"], l + 1)
                dve.wait_ge(s["kx_e"], 2 * l + 2)
                for h in range(2):
                    p = slice(64 * h, 64 * h + 64)
                    V.tensor_tensor(qfP[p, :, h, :], bqT[p, :, :], dec0[p, :, :], ALU.mult)
                    V.tensor_tensor(qxP[p, :, h, :], bqT[p, :, P:T], dec1[p, :, 0:P], ALU.mult)
                V.tensor_tensor(kx[:], kx[:], bkT[:, :, 0:P], ALU.mult)
                for pr in range(2):
                    dve.wait_ge(s["ke"], 2 * l + pr + 1)
                    k = bkT[:, pr, :].rearrange("p (a n) -> p a n", a=2).unsqueeze(2).broadcast_to([P, 2, NBLK, P])
                    last = V.tensor_tensor(kfac[:, pr], kfac[:, pr], k, ALU.mult)
                last.then_inc(s["gla_in"], 1)

            def mixer(l):
                ph = 2 * l
                modulate(ph)
                low_of_tokens(ph)
                for u in range(NIN + 2):
                    low_unit(l, u)
                    if l == 0:
                        condition_rows(unit_rows(u))
                    if l == 0 and u == U_BA + 2:
                        dve.wait_ge(s["evac"], U_BA + 1)
                        for a in (2, 3):
                            conditioning(0, a, bank[4 + U_BA % 4][:, T + a * KT:T + (a + 1) * KT]).then_inc(s["modT"], 1)
                    if u == U_AQ1:
                        dve.wait_ge(s["evac"], l * NIN + 3)
                        indexer(l)
                    if u == U_AKV:
                        select(0)
                    if u == U_BQ:
                        select(1)
                    if u == U_BG0:
                        decay(l)
                    if u == U_BG1:
                        decay_products(l)
                for tb in range(2):
                    dve.wait_ge(s["at_ps"], 3 * l + tb + 1)
                    V.tensor_tensor(at_sb[:, tb, :].rearrange("p (h t) -> p h t", h=4),
                                    bank[tb][:].rearrange("p (h t) -> p h t", h=4),
                                    upper_eq[:].unsqueeze(1).broadcast_to([P, 4, P]), ALU.mult).then_inc(s["at_msk"], 1)
                for k, (t, heads, keys) in enumerate(HEAD_GROUPS):
                    dve.wait_ge(s["lg_ps"], l * NG + k + 1)
                    for i, h in enumerate(heads):
                        last = V.scalar_tensor_tensor(out=prob[t][:, h, :], in0=dsel[t][:], scalar=2.0 ** -(h + 1),
                                                      in1=bank[4 + k % 4][:, i * keys:(i + 1) * keys],
                                                      op0=ALU.mult, op1=ALU.add)
                    last.then_inc(s["lg_sb"], 1)
                    if k in (1, NG - 1):
                        dve.wait_ge(s["lg_sb"], l * NG + k + 1)
                        V.tensor_reduce(nmax[:, t, :], prob[t][:], AX.X, ALU.max, negate=True).then_inc(s["nmax"], 1)
                dve.wait_ge(s["evac"], l * NIN + NIN)
                dve.wait_ge(s["wa2_ld"], 32 * (l + 1))
                for t in range(TT):
                    g = sbg[:, t, :].rearrange("p (h e) -> p h e", h=B_HEADS)
                    last = V.tensor_tensor(g, g, gnorm[:].unsqueeze(1).broadcast_to([P, B_HEADS, B_DV]), ALU.mult)
                link(last)
                for t in range(TT):
                    ob = bank[3] if t == 0 else bank[0]
                    dve.wait_ge(s["rms"], l * TT + t + 1)
                    for h in range(B_HEADS):
                        e = slice(h * B_DV, (h + 1) * B_DV)
                        V.scalar_tensor_tensor(out=ycat[:, t, 512 + h * B_DV:512 + (h + 1) * B_DV], in0=ob[:, e],
                                               scalar=rms[:, t, h:h + 1], in1=sbg[:, t, e], op0=ALU.mult, op1=ALU.mult)
                for t in range(TT):
                    dve.wait_ge(s["pv_ps"], l * TT + t + 1)
                    link(V.reciprocal(rinv[:, t, :], rsum[:, t, :]))
                    last = V.tensor_tensor(ycat[:, t, 0:512].rearrange("p (h e) -> p h e", h=A_HEADS),
                                           bank[6 + t][:].rearrange("p (h e) -> p h e", h=A_HEADS),
                                           rinv[:, t, :].unsqueeze(2).broadcast_to([P, A_HEADS, 64]), ALU.mult)
                last.then_inc(s["ycat"], 1)
                if l == 0:
                    dve.wait_ge(s["mod_ps"], 5)
                    for a in (4, 5):
                        conditioning(0, a, bank[5][:, a * KT:(a + 1) * KT]).then_inc(s["modT"], 1)
                for b in range(4):
                    dve.wait_ge(s["yT_H"], 4 * l + b + 1)
                    k = slice(2 * b, 2 * b + 2)
                    V.tensor_tensor(hT_L[:, k, :], bank[b][:].rearrange("p (a t) -> p a t", a=2),
                                    hT_H[:, k, :].bitcast(F32), ALU.subtract).then_inc(s["yT_L"], 1)
                dve.wait_ge(s["modT"], 5 if l == 0 else 11)
                gate_diag(ph, prob0[:].rearrange("p h t -> p (h t)"))
                for u in range(NIN + 2, NU):
                    low_unit(l, u)

                def terms(t):
                    for v in range(4):
                        if t == 0:
                            dve.wait_ge(s["proj"], l * NU + NIN + v + 1)
                        cc = slice(v * 256, (v + 1) * 256)
                        last = V.tensor_tensor(ycat[:, t, cc], bank[4 + v][:, t * 256:(t + 1) * 256], g_row[:, cc], ALU.mult)
                    link(last)
                layer_norm(ph, terms)

            mixer(0)

            def dense_low_gu(q):
                for i, raw in enumerate((raw_g, raw_u)):
                    cc = slice(i * FC, (i + 1) * FC)
                    dve.wait_ge(s["f_guH"], 2 * q + i + 1)
                    V.tensor_tensor(gu_L[q % 2][:, :, cc], raw[q % 2][:], gu_H[q % 2][:, :, cc].bitcast(F32), ALU.subtract)\
                        .then_inc(s["f_guL"], 1)

            gate_diag(1, ycat[:, 0, :])
            dense_low_gu(0)
            modulate(1)
            low_of_tokens(1)
            condition_rows(step_rows(-1))
            for q in range(STEPS + 1):
                p = q - 1
                if q + 1 < STEPS:
                    dense_low_gu(q + 1)
                if q < STEPS:
                    dve.wait_ge(s["f_silu"], 2 * q + 1)
                    if q >= 1:
                        dve.wait_ge(s["f_t"], 2 * p + 1)
                    V.tensor_tensor(hid[:, 0, :], silu_g[:, 0, :], bank[0][:, FC:2 * FC], ALU.mult).then_inc(s["f_hid"], 1)
                if q >= 1:
                    for j in range(2):
                        dve.wait_ge(s["f_dH"], 2 * p + j + 1)
                        V.tensor_tensor(d_L[:, j, :], raw_d[p % 2][:, j, :], d_H[:, j, :].bitcast(F32), ALU.subtract)\
                            .then_inc(s["f_dL"], 1)
                    dve.wait_ge(s["f_tH"], 2 * p + 2)
                    V.tensor_tensor(hidT_L[:, 1], bank[7][:, 0:256].rearrange("p (a t) -> p a t", a=2),
                                    hidT_H[:, 1].bitcast(F32), ALU.subtract).then_inc(s["f_tL"], 1)
                if q < STEPS:
                    dve.wait_ge(s["f_silu"], 2 * q + 2)
                    if q >= 1:
                        dve.wait_ge(s["f_t"], 2 * p + 2)
                    V.tensor_tensor(hid[:, 1, :], silu_g[:, 1, :], bank[1][:, FC:2 * FC], ALU.mult).then_inc(s["f_hid"], 1)
                    condition_rows(step_rows(q))
                    dve.wait_ge(s["f_tH"], 2 * q + 1)
                    if q in MOD_AT_STEP:
                        conditioning(1, MOD_AT_STEP[q], bank[4][:, T:T + KT]).then_inc(s["modT"], 1)
                    V.tensor_tensor(hidT_L[:, 0], bank[4][:, 0:256].rearrange("p (a t) -> p a t", a=2),
                                    hidT_H[:, 0].bitcast(F32), ALU.subtract).then_inc(s["f_tL"], 1)

            def dense_terms(t):
                if t == 0:
                    dve.wait_ge(s["f_d"], 4 * STEPS)
                for h in range(2):
                    cc = slice(h * 512, (h + 1) * 512)
                    last = V.tensor_tensor(ycat[:, t, cc], bank[(2, 5)[t] + h][:], g_row[:, cc], ALU.mult)
                link(last)
            layer_norm(1, dense_terms)
            dve.wait_ge(s["mod_ps"], 11)
            conditioning(1, 5, bank[4][:, T:T + KT]).then_inc(s["modT"], 1)

            mixer(1)

            V.memset(tick[:, 0:1], 0.0).then_inc(s["m_guL"], 4)
            V.memset(tick[:, 1:2], 0.0).then_inc(s["m_dL"], 4)
            V.memset(tick[:, 2:3], 0.0).then_inc(s["m_hid"], 2)
            V.memset(tick[:, 3:4], 0.0).then_inc(s["m_tL"], 1)
            V.memset(tick[:, 4:5], 0.0).then_inc(s["m_yL"], 2)
            V.memset(tick[:, 5:6], 0.0).then_inc(s["m_S"], 1)
            modulate(3)
            dve.wait_ge(s["rt_ps"], 1)
            dve.wait_ge(s["small_ld"], 32)
            lg, cand, oh1, lg2, oh2, tmp, gate = rt[0], rt[1], rt[2], rt[3], rt[4], rt[5], rt[6]
            rank, sel, rank_m = rt[7], rt[8], rt[9]

            def wide(v):
                return v.unsqueeze(2).broadcast_to([P, TT, NE])
            rev = rev8[:].unsqueeze(1).broadcast_to([P, TT, NE])
            link(V.tensor_tensor(lg[:], bank[7][:, 0:16].rearrange("p (t e) -> p t e", t=2),
                                 br_row[:].unsqueeze(1).broadcast_to([P, TT, NE]), ALU.add))

            def first_highest(src, value, mark):
                link(V.tensor_reduce(value, src[:], AX.X, ALU.max))
                link(V.tensor_tensor(cand[:], src[:], wide(value), ALU.is_equal))
                link(V.tensor_tensor(cand[:], cand[:], rev, ALU.mult))
                link(V.tensor_reduce(v2[:, 5, :], cand[:], AX.X, ALU.max))
                link(V.tensor_tensor(mark[:], cand[:], wide(v2[:, 5, :]), ALU.is_equal))
            first_highest(lg, v2[:, 0, :], oh1)
            link(V.scalar_tensor_tensor(out=lg2[:], in0=oh1[:], scalar=FILL, in1=lg[:], op0=ALU.mult, op1=ALU.add))
            first_highest(lg2, v2[:, 1, :], oh2)
            V.tensor_tensor(sel[:], oh1[:], oh2[:], ALU.add).then_inc(s["sel"], 1)
            V.tensor_tensor(v2[:, 2, :], v2[:, 1, :], v2[:, 0, :], ALU.subtract).then_inc(s["lg8"], 1)
            dve.wait_ge(s["expd"], 1)
            link(V.tensor_scalar(v2[:, 4, :], v2[:, 3, :], 1.0, None, ALU.add))
            link(V.reciprocal(v2[:, 0, :], v2[:, 4, :]))
            link(V.tensor_tensor(v2[:, 1, :], v2[:, 3, :], v2[:, 0, :], ALU.mult))
            V.tensor_tensor(tmp[:], oh1[:], wide(v2[:, 0, :]), ALU.mult)
            link(V.tensor_tensor(gate[:], oh2[:], wide(v2[:, 1, :]), ALU.mult))
            link(V.memset(gate_tab[:], 0.0))
            for p in range(2):
                last = V.tensor_tensor(gate_tab[:, :, 1 + p * NE:1 + (p + 1) * NE], gate[:], tmp[:], ALU.add)
            dve.wait_ge(s["sel"], 1)
            dve.wait_ge(s["rank_ps"], 1)
            link(V.tensor_scalar(rank[:], bank[7][:, 16:32].rearrange("p (t e) -> p t e", t=2), 1.0, None, ALU.add))
            link(V.tensor_tensor(rank_m[:], rank[:], sel[:], ALU.mult))
            link(V.memset(rank_tab[:], -1.0))
            V.tensor_scalar(rank_tab[:, :, 0:NE], rank_m[:], -1.0, None, ALU.add)
            link(V.tensor_scalar(rank_tab[:, :, NE:2 * NE], rank_m[:], -1.0 - P, None, ALU.add))
            link(V.tensor_reduce(npass_f[:, 0:1], bank[7][:, 32:40], AX.X, ALU.max))
            link(V.tensor_scalar(npass_f[:, 1:2], npass_f[:, 0:1], float(P), 1.0, ALU.is_gt, ALU.add))
            V.tensor_copy(npass_i[:], npass_f[:, 1:2]).then_inc(s["npass"], 1)

            def one_hot(col):
                for t in range(TT):
                    V.tensor_scalar(one_G[:, t, :], slot_id[:], rank_tab[:, t, col], None, ALU.is_equal).then_inc(s["G"], 1)
            one_hot(slice(0, 1))
            for t in range(TT):
                dve.wait_ge(s["xsplit"], t + 1)
                V.tensor_tensor(xL[t][:], x_sb[:, t, :], xH[t][:].bitcast(F32), ALU.subtract).then_inc(s["xsplitL"], 1)

            V.memset(ycat[:], 0.0).then_inc(s["m_acc"], 4)

            def moe_low_gu(q, it2):
                for i, raw in enumerate((raw_g, raw_u)):
                    cc = slice(i * FC, (i + 1) * FC)
                    dve.wait_ge(s["m_guH"], it2 * (4 * STEPS) + (2 * q + i + 1))
                    V.tensor_tensor(gu_L[q % 2][:, :, cc], raw[q % 2][:], gu_H[q % 2][:, :, cc].bitcast(F32), ALU.subtract)\
                        .then_inc(s["m_guL"], 1)

            def low_gathered():
                V.tensor_tensor(xgL, xg_full[:], xgH.bitcast(F32), ALU.subtract).then_inc(s["xg_L"], 1)

            def moe_low_down(q, it2):
                for j in range(2):
                    dve.wait_ge(s["m_dH"], it2 * (4 * STEPS) + (2 * q + j + 1))
                    V.tensor_tensor(d_L[:, j, :], raw_d[q % 2][:, j, :], d_H[:, j, :].bitcast(F32), ALU.subtract)\
                        .then_inc(s["m_dL"], 1)
                dve.wait_ge(s["m_tH"], it2 * (2 * STEPS) + (q + 1))
                V.tensor_tensor(hidT_L[:, 0], bank[4][:, 0:256].rearrange("p (a t) -> p a t", a=2),
                                hidT_H[:, 0].bitcast(F32), ALU.subtract).then_inc(s["m_tL"], 1)

            def accumulate(E):
                dve.wait_ge(s["m_acc"], E * 4 + 4)
                for i, b in enumerate((5, 6, 7, 2)):
                    t, h = i // 2, i % 2
                    a = ycat[:, t, h * 512:(h + 1) * 512]
                    dve.wait_ge(s["m_sc"], E * 4 + (i + 1))
                    V.scalar_tensor_tensor(out=a, in0=bank[b][:], scalar=gate_tab[:, t, bass.ds(E, 1)], in1=a,
                                           op0=ALU.mult, op1=ALU.add).then_inc(s["m_acc"], 1)

            moe_low_gu(0, 0)
            dve.wait_ge(s["xg_H"], 1)
            low_gathered()
            dve.wait_ge(s["npass"], 1)
            npass = dve.value_load(npass_i[0:1, 0:1], min_val=1, max_val=2)
            with dve.Fori(0, npass) as ps:
                with dve.Fori(0, NE // 2) as pair:
                    it2 = ps * (NE // 2) + pair
                    for par in range(2):
                        E = it2 * 2 + par
                        for st in range(STEPS):
                            q = par * STEPS + st
                            moe_low_gu(q + 1, it2)
                            if st == 0:
                                accumulate(E)
                            dve.wait_ge(s["m_silu"], it2 * (2 * STEPS) + (q + 1))
                            dve.wait_ge(s["m_t"], it2 * (2 * STEPS) + (q + 1))
                            V.tensor_tensor(hid[:, 0, :], silu_g[:, 0, :], bank[q % 2][:, FC:2 * FC], ALU.mult)\
                                .then_inc(s["m_hid"], 1)
                            if st >= 1:
                                moe_low_down(q - 1, it2)
                            if st == 2:
                                dve.wait_ge(s["m_st"], E + 1)
                                V.tensor_copy(one_S[:], bank[7][:, 0:T]).then_inc(s["m_S"], 1)
                            if st == 3:
                                one_hot(bass.ds(E + 1, 1))
                        moe_low_down(par * STEPS + STEPS - 1, it2)
                        dve.wait_ge(s["xg_H"], E + 2)
                        low_gathered()
                        for h in range(2):
                            dve.wait_ge(s["m_yH"], E * 2 + (h + 1))
                            cc = slice(h * 512, (h + 1) * 512)
                            V.tensor_tensor(yL[:, cc], bank[2 + h][:], yH[:, cc].bitcast(F32), ALU.subtract)\
                                .then_inc(s["m_yL"], 1)
            n_done = npass * NE
            accumulate(n_done)
            dve.wait_ge(s["m_acc"], n_done * 4 + 8)
            dve.wait_ge(s["xg_L"], n_done + 1)
            V.memset(v2[:, 4, 0:1], 0.0).then_inc(s["m_end"], 1)
            gate_diag(3, xg_full[:].rearrange("p k t -> p (k t)"))

            def moe_terms(t):
                link(V.tensor_tensor(ycat[:, t, :], ycat[:, t, :], g_row[:], ALU.mult))
            layer_norm(3, moe_terms)


_INS = ["x", "c", "w_in", "w_a2", "b_a", "gla_norm_g", "w_out", "w_mod", "b_mod", "ln_g", "ln_b",
        "ffn_w_gate", "ffn_w_up", "ffn_w_down", "w_router", "b_router", "moe_w_gate", "moe_w_up", "moe_w_down"]
_OUTS = [((1, T, D), "float32")]


def kernel(**inputs):
    import numpy as np
    import concourse.bacc as bacc
    from concourse.bass_utils import run_bass_kernel_spmd

    nc = bacc.Bacc("TRN2", target_bir_lowering=False, num_devices=1)
    arrays, args = {}, []
    for name in _INS:
        a = np.ascontiguousarray(inputs[name])
        arrays[f"in_{name}_dram"] = a
        args.append(nc.dram_tensor(f"in_{name}_dram", a.shape, mybir.dt.from_np(a.dtype), kind="ExternalInput").ap())
    for i, (shape, dtype) in enumerate(_OUTS):
        args.append(nc.dram_tensor(f"out_{i}_dram", shape, mybir.dt.from_np(np.dtype(dtype)), kind="ExternalOutput").ap())
    hybrid_decoder(nc, *args)
    r = run_bass_kernel_spmd(nc, [arrays], core_ids=[0])
    return r.results[0]["out_0_dram"]
```

```python
from contextlib import ExitStack

import concourse.bass as bass
from concourse import mybir

F32 = mybir.dt.float32
F32R = mybir.dt.float32r
I32 = mybir.dt.int32
ALU = mybir.AluOpType
ACT = mybir.ActivationFunctionType
AX = mybir.AxisListType

P = 128
D = 1024
KT = D // P
T = 256
TT = T // P
DEPTH = 2
A_HEADS = 8
TOPK = min(256, T // 4)
B_HEADS = 4
B_DV = 128
RANK = 16
D_FF = 2816
FC = 256
STEPS = D_FF // FC
NE = 8
GATHER_AT = (7, 9)
UNITC = 256
ALPHA = (2 * DEPTH) ** 0.25
EPS = 1e-5
NEG = -1.0e30
FILL = -1.0e38
TAKEN = -3.0e38
SQ = 64 ** -0.5
BLK = 32
NBLK = P // BLK

AQ, AK, AV, IQ, IK, IW, BQ, BK, BV, BG, BA = 0, 512, 576, 640, 1152, 1216, 1224, 1480, 1736, 2248, 2760
U_IQ0, U_IQ1, U_IKW, U_AQ0, U_AQ1, U_AKV, U_BQ, U_BK, U_BA, U_BV0, U_BV1, U_BG0, U_BG1 = range(13)
W_IN_UNITS = [(IQ, 256), (IQ + 256, 256), (IK, 72), (AQ, 256), (AQ + 256, 256), (AK, 128), (BQ, 256),
              (BK, 256), (BA, RANK), (BV, 256), (BV + 256, 256), (BG, 256), (BG + 256, 256)]
NIN = len(W_IN_UNITS)
NU = NIN + D // UNITC
MOD_ROWS = [(l, a, k) for l in range(DEPTH) for a in range(0 if l else 2, 6) for k in range(KT)]
ROWS_L0 = 4 * KT
ROWS_AT_UNIT = {1: 3, 2: 3, 3: 3, 4: 3, 5: 4, 10: 3, 11: 3, 12: 3, 13: 3, 14: 4}
ROWS_STEP = 5
MOD_AT_STEP = {(8 * (a + 1) + 4) // 5 + 1: a for a in range(5)}
HEAD_GROUPS = [(0, range(0, 4), 128), (0, range(4, 8), 128)] + [(1, range(2 * g, 2 * g + 2), 256) for g in range(4)]
NG = len(HEAD_GROUPS)


def hybrid_decoder(nc, x, c, w_in, w_a2, b_a, gla_norm_g, w_out, w_mod, b_mod, ln_g, ln_b,
                   ffn_w_gate, ffn_w_up, ffn_w_down, w_router, b_router,
                   moe_w_gate, moe_w_up, moe_w_down, out):
    ctx = ExitStack()
    with ctx:
        top = [16640]

        def place(name, shape, dt=F32, at=None):
            size = 4
            for n in shape[1:]:
                size *= n
            size = (size + 31) // 32 * 32
            if at is None:
                at = top[0]
                top[0] += size
            return nc.alloc_sbuf_tensor_at(name, shape, dt, offset=at)

        def sem(name):
            return ctx.enter_context(nc.semaphore(name))

        x_sb = place("x_sb", [P, TT, D])
        hT_H = place("hT_H", [P, KT, T], F32R)
        hT_L = place("hT_L", [P, KT, T], F32R)
        hfull_at = top[0]
        hfull = place("hfull", [P, KT, T])
        ycat_at = top[0]
        ycat = place("ycat", [P, TT, D])
        rows_at = top[0]
        g_row = place("g_row", [P, D])
        lng_row = place("lng_row", [P, D])
        lnb_row = place("lnb_row", [P, D])
        hidT_at = top[0]
        hidT_H = place("hidT_H", [P, 2, 2, P], F32R)
        hidT_L = place("hidT_L", [P, 2, 2, P], F32R)
        hid = place("hid", [P, 2, FC])
        silu_g = place("silu_g", [P, 2, FC])
        ident = place("ident", [P, P])
        ones = place("ones", [P, T])
        upper = place("upper", [P, P])
        upper_eq = place("upper_eq", [P, P])
        dist = place("dist", [P, T])
        ahead = place("ahead", [P, T])
        slot_id = place("slot_id", [P, P])
        rev8 = place("rev8", [P, NE])
        half_neg = place("half_neg", [P, 8])
        stage_at = top[0]
        stage = place("stage", [P, P])
        stage2 = place("stage2", [P, P])
        ln_cols = place("ln_cols", [P, 64])
        cols = place("cols", [P, P])
        modT = place("modT", [P, DEPTH * 48])
        ln_mod = place("ln_mod", [P, 3, 2, KT], at=stage_at)
        c_act = place("c_act", [P, KT])
        stats = place("stats", [P, TT, 2, 6])
        mv = place("mv", [P, TT, 2])
        veps = place("veps", [P, TT])
        rstd = place("rstd", [P, TT])
        shift_n = place("shift_n", [P, TT])
        iw = place("iw", [P, TT, 8])
        top8 = place("top8", [P, 8])
        nmax = place("nmax", [P, TT, A_HEADS])
        rsum = place("rsum", [P, TT, A_HEADS])
        rinv = place("rinv", [P, TT, A_HEADS])
        ssq = place("ssq", [P, TT, B_HEADS])
        rms = place("rms", [P, TT, B_HEADS])
        gnorm = place("gnorm", [P, B_DV])
        nb127 = place("nb127", [P, 2])
        wr = place("wr", [P, KT, NE])
        br_row = place("br_row", [P, NE])
        raw_g0 = place("raw_g0", [P, KT, FC])
        raw_u0 = place("raw_u0", [P, KT, FC])
        gu_H0 = place("gu_H0", [P, KT, 2 * FC], F32R)
        gu_L0 = place("gu_L0", [P, KT, 2 * FC], F32R)
        over = top[0]
        raw_g1 = place("raw_g1", [P, KT, FC])
        raw_u1 = place("raw_u1", [P, KT, FC])
        raw_d0 = place("raw_d0", [P, 2, D])
        raw_d1 = place("raw_d1", [P, 2, D])
        d_H = place("d_H", [P, 2, D], F32R)
        d_L = place("d_L", [P, 2, D], F32R)
        gu_H1 = place("gu_H1", [P, KT, 2 * FC], F32R)
        gu_L1 = place("gu_L1", [P, KT, 2 * FC], F32R)
        end = top[0]
        raw_g, raw_u, raw_d = [raw_g0, raw_g1], [raw_u0, raw_u1], [raw_d0, raw_d1]
        gu_H, gu_L = [gu_H0, gu_H1], [gu_L0, gu_L1]
        top[0] = over
        aqT = place("aqT", [P, 4, T])
        iqT = place("iqT", [P, 4, T])
        akP = place("akP", [P, 2, T])
        ikP = place("ikP", [P, 2, T])
        av = place("av", [P, TT, 64])
        bqT = place("bqT", [P, 2, T])
        bkT = place("bkT", [P, 2, T])
        baT = place("baT", [P, T])
        wa2 = place("wa2", [P, T])
        bT = place("bT", [P, 2, T])
        dec0 = place("dec0", [P, 2, T])
        dec1 = place("dec1", [P, 2, T])
        bv = place("bv", [P, TT, 512])
        sbg = place("sbg", [P, TT, 512])
        score0 = place("score0", [P, P])
        score1 = place("score1", [P, T])
        relu_a = place("relu_a", [P, 512])
        relu_b = place("relu_b", [P, 512])
        dsel0 = place("dsel0", [P, P])
        dsel1 = place("dsel1", [P, T])
        prob0 = place("prob0", [P, A_HEADS, P])
        prob1 = place("prob1", [P, A_HEADS, T])
        pT0 = place("pT0", [P, 8, P])
        kfac = place("kfac", [P, 2, 2, NBLK, P])
        qfP = place("qfP", [P, 2, 2, T])
        qxP = place("qxP", [P, 2, 2, P])
        kx = place("kx", [P, 2, P])
        at_sb = place("at_sb", [P, 3, 512])
        assert top[0] <= end, (top[0] - end)
        assert end <= 229344, end
        pT1 = place("pT1", [P, 16, P], at=hfull_at)
        top[0] = end
        one_G = place("one_G", [P, TT, P], F32R)
        one_S = place("one_S", [P, T], F32R)
        rank_tab = place("rank_tab", [P, TT, 2 * NE + 1])
        gate_tab = place("gate_tab", [P, TT, 2 * NE + 1])
        rt = [place(f"rt{i}", [P, TT, NE]) for i in range(10)]
        v2 = place("v2", [P, 6, TT])
        tick = place("tick", [P, 8])
        npass_f = place("npass_f", [P, 2])
        npass_i = place("npass_i", [P, 1], I32)
        assert top[0] <= 229344, top[0]
        spare_at = top[0]
        mod_first = place("mod_first", [P, KT, 2 * D], at=over)
        top[0] = spare_at
        mod_acc = [place(f"mod_acc{i}", [P, D]) for i in range(2)]
        assert top[0] <= 229344, top[0]
        mod_ring = [[place(f"mod_row{l}{i}", [P, D], at=(ycat_at if i >= 2 else hfull_at if l else hidT_at) + 4 * D * (i % 2))
                     for i in range(4)] for l in range(DEPTH)]

        score, dsel, prob, relu = [score0, score1], [dsel0, dsel1], [prob0, prob1], [relu_a, relu_b]
        xH0 = place("xH0", [P, D], F32R, at=rows_at)
        xH1 = place("xH1", [P, D], F32R, at=rows_at + 4096)
        xL0 = place("xL0", [P, D], F32R, at=rows_at + 8192)
        xL1 = place("xL1", [P, D], F32R, at=hfull_at + 4096)
        xH, xL = [xH0, xH1], [xL0, xL1]
        yH = place("yH", [P, D], F32R, at=hfull_at)
        yL = place("yL", [P, D], F32R, at=spare_at)

        def half(tokens, i):
            return tokens[:, 4 * i:4 * i + 4, :].rearrange("p a b -> p (a b)").rearrange("p (k n) -> p k n", k=KT)
        xgH = [half(hT_H, i) for i in range(2)]
        xgL = [half(hT_L, i) for i in range(2)]
        gate3_row = mod_acc[1]

        bank = [ctx.enter_context(nc.psum_tensor(f"bank{i}", [P, 512], F32)) for i in range(8)]

        s = {}
        for name in """const x_ld stage_ld stage2_ld small_ld rows_ld wa2_ld pads stageT cols_rd cact mod_sum row_rd mod_ps modT x_ln xT_ps hfull hT_H hT_L
            gdiag g_ps g_row wH wL proj evac idx_ps relu idxacc dve_chain act_chain pool_chain z_ps az decay
            qe ke kx_e kfac_rd gla_in at_ps at_sb at_msk o_ps ssq rms lg_ps lg_sb nmax pexp pt_ps pt_sb pv_ps ycat
            yT_ps yT_H yT_L mv rstd x_n ln_cols stored
            f_guH f_guL f_gu f_silu f_hid f_t f_tH f_tL f_dH f_dL f_d
            rt_ps lg8 expd sel rank_ps npass rdiag r_ps xmod xsplit xsplitL zeros G xg_ps xg_H xg_L
            m_guH m_guL m_gu m_silu m_hid m_t m_tH m_tL m_dH m_dL m_d m_st m_S m_sc m_acc m_yH m_yL m_end""".split():
            s[name] = sem("s_" + name)
        mod_ld = [sem(f"s_mod_ld{i}") for i in range(KT)]
        row_ld = [sem(f"s_row_ld{i}") for i in range(4)]
        w_ld = [sem(f"s_w_ld{i}") for i in range(2)]
        f_ld = {k: [sem(f"s_f_ld_{k}{i}") for i in range(2)] for k in "gud"}
        m_ld = {k: [sem(f"s_m_ld_{k}{i}") for i in range(2)] for k in "gud"}

        block = ctx.enter_context(nc.Block())

        def unit_rows(u):
            n = sum(ROWS_AT_UNIT[v] for v in ROWS_AT_UNIT if v < u)
            return range(n, n + ROWS_AT_UNIT.get(u, 0))

        def step_rows(q):
            n = ROWS_L0 + ROWS_STEP * (q - 1)
            return range(n, min(n + ROWS_STEP, len(MOD_ROWS))) if q >= 1 else range(0)

        def mm3(out_ap, aH, aL, bH, bL, first, last):
            nc.tensor.matmul(out_ap, aH, bH, start=first, stop=False)
            nc.tensor.matmul(out_ap, aH, bL, start=False, stop=False)
            return nc.tensor.matmul(out_ap, aL, bH, start=False, stop=last)

        def unit_src(l, u):
            if u < NIN:
                a, n = W_IN_UNITS[u]
                return w_in[l, :, a:a + n].rearrange("(k p) f -> p k f", p=P), n
            a = (u - NIN) * UNITC
            return w_out[l, :, a:a + UNITC].rearrange("(k p) f -> p k f", p=P), UNITC

        wraw = [raw_g0, raw_u0]

        @block.sync
        def _(sp):
            for k in range(KT):
                sp.dma_start(mod_first[:, k, :], w_mod[0, k * P:(k + 1) * P, 0:2 * D]).then_inc(mod_ld[k], 16)
                if k >= KT - TT:
                    t = k - (KT - TT)
                    sp.dma_start(x_sb[:, t, :], x[0, t * P:(t + 1) * P, :]).then_inc(s["x_ld"], 16)

            def load_mod_rows(rows):
                for n in rows:
                    l, a, k = MOD_ROWS[n]
                    if n >= 4:
                        sp.wait_ge(s["row_rd"], n - 3)
                    else:
                        sp.wait_ge(s["mod_ps"], 1)
                    if n == ROWS_L0:
                        sp.wait_ge(s["hT_L"], 4)
                        sp.wait_ge(s["g_ps"], 4)
                        sp.wait_ge(s["x_ln"], 2)
                    sp.dma_start(mod_ring[l][n % 4][:], w_mod[l, k * P:(k + 1) * P, a * D:(a + 1) * D])\
                        .then_inc(row_ld[n % 4], 16)

            def mixer_loads(l):
                for u in range(NU):
                    if u >= 2:
                        sp.wait_ge(s["wL"], l * NU + u - 1)
                    elif l:
                        sp.wait_ge(s["f_guL"], 2 * STEPS)
                    src, n = unit_src(l, u)
                    sp.dma_start(wraw[u % 2][:, :, 0:n], src).then_inc(w_ld[u % 2], 16)
                    if l == 0:
                        load_mod_rows(unit_rows(u))

            mixer_loads(0)

            def dense_gu(q):
                if q == 0:
                    sp.wait_ge(s["wL"], NU)
                elif q == 1:
                    sp.wait_ge(s["yT_L"], 4)
                else:
                    sp.wait_ge(s["f_guL"], 2 * (q - 1))
                f = slice(q * FC, (q + 1) * FC)
                sp.dma_start(raw_g[q % 2][:], ffn_w_gate[0, :, f].rearrange("(k p) f -> p k f", p=P)).then_inc(f_ld["g"][q % 2], 16)
                sp.dma_start(raw_u[q % 2][:], ffn_w_up[0, :, f].rearrange("(k p) f -> p k f", p=P)).then_inc(f_ld["u"][q % 2], 16)

            dense_gu(0)
            dense_gu(1)
            for q in range(STEPS):
                if 1 <= q < STEPS - 1:
                    dense_gu(q + 1)
                if q >= 2:
                    sp.wait_ge(s["f_dL"], 2 * (q - 1))
                sp.dma_start(raw_d[q % 2][:], ffn_w_down[0, q * FC:(q + 1) * FC, :].rearrange("(k p) f -> p k f", p=P))\
                    .then_inc(f_ld["d"][q % 2], 16)
                load_mod_rows(step_rows(q))
            mixer_loads(1)

            mg, mu, md = moe_w_gate[0], moe_w_up[0], moe_w_down[0]
            sp.wait_ge(s["wL"], 2 * NU)
            sp.wait_ge(s["yT_L"], 8)

            def load_gate_up(e, st, slot, rows_split=None):
                f = slice(st * FC, (st + 1) * FC)
                sp.dma_start(raw_g[slot][:], mg[e, :, f].rearrange("(k p) f -> p k f", p=P)).then_inc(m_ld["g"][slot], 16)
                if rows_split is not None:
                    sp.wait_ge(s["m_dL"], rows_split)
                sp.dma_start(raw_u[slot][:], mu[e, :, f].rearrange("(k p) f -> p k f", p=P)).then_inc(m_ld["u"][slot], 16)

            def load_down(e, st, slot):
                sp.dma_start(raw_d[slot][:], md[e, st * FC:(st + 1) * FC, :].rearrange("(k p) f -> p k f", p=P))\
                    .then_inc(m_ld["d"][slot], 16)

            def expert_pair(pair, it2, following):
                for par in range(2):
                    for st in range(STEPS):
                        q = par * STEPS + st
                        rows_split = it2 * (4 * STEPS) + (2 * q + 4)
                        sp.wait_ge(s["m_guL"], it2 * (4 * STEPS) + (2 * q + 4))
                        if st < STEPS - 1:
                            load_gate_up(pair * 2 + par, st + 1, (q + 1) % 2, rows_split if q == 0 else None)
                        else:
                            load_gate_up(pair * 2 + 1 if par == 0 else following, 0, (q + 1) % 2)
                        if q:
                            sp.wait_ge(s["m_dL"], rows_split)
                        load_down(pair * 2 + par, st, q % 2)

            load_gate_up(0, 0, 0)
            load_down(0, 0, 1)
            last = NE // 2 - 1
            with sp.Fori(0, last) as pair:
                expert_pair(pair, pair, pair * 2 + 2)
            expert_pair(last, last, 0)
            sp.wait_ge(s["npass"], 1)
            npass = sp.value_load(npass_i[0:1, 0:1], min_val=1, max_val=2)
            with sp.If(npass > 1):
                with sp.Fori(0, last) as pair:
                    expert_pair(pair, pair + NE // 2, pair * 2 + 2)
                expert_pair(last, last + NE // 2, 0)
            for t in range(TT):
                sp.wait_ge(s["x_ln"], 7 + t)
                sp.dma_start(out[0, t * P:(t + 1) * P, :], x_sb[:, t, :]).then_inc(s["stored"], 16)
            sp.wait_ge(s["stored"], 16 * TT)

        @block.gpsimd
        def _(pool):
            n = [0]

            def link(ins):
                n[0] += 1
                ins.then_inc(s["pool_chain"], 1)
                pool.wait_ge(s["pool_chain"], n[0])

            link(pool.memset(stage[:], 0.0))
            pool.dma_start(stage[0:96, :], b_mod.rearrange("l (j p) -> (l j) p", p=P)).then_inc(s["stage_ld"], 16)
            pool.dma_start(stage[96:104, :], c.rearrange("a (j p) -> (a j) p", p=P)).then_inc(s["stage_ld"], 16)
            pool.dma_start(stage[104:108, :], b_a.rearrange("l (j p) -> (l j) p", p=P)).then_inc(s["stage_ld"], 16)
            pool.dma_start(wr[:], w_router[0].rearrange("(k p) e -> p k e", p=P)).then_inc(s["small_ld"], 16)
            pool.dma_start(br_row[:], b_router[0:1, :].broadcast_to([P, NE])).then_inc(s["small_ld"], 16)
            link(pool.memset(ident[:], 0.0))
            link(pool.affine_select(out=ident[:], in_=ident[:], compare_op=ALU.not_equal, fill=1.0, base=0,
                                    pattern=[[-1, P]], channel_multiplier=1))
            link(pool.memset(ones[:], 1.0))
            pool.affine_select(out=upper[:], in_=ones[:, 0:P], compare_op=ALU.is_gt, fill=0.0, base=0,
                               pattern=[[1, P]], channel_multiplier=-1)
            pool.affine_select(out=upper_eq[:], in_=ones[:, 0:P], compare_op=ALU.is_ge, fill=0.0, base=0,
                               pattern=[[1, P]], channel_multiplier=-1)
            link(pool.iota(dist[:], pattern=[[1, T]], base=-P, channel_multiplier=-1, allow_small_or_imprecise_dtypes=True))
            link(pool.affine_select(out=dist[:], in_=dist[:], compare_op=ALU.is_ge, fill=NEG, base=P,
                                    pattern=[[-1, T]], channel_multiplier=1))
            link(pool.memset(ahead[:], 0.0))
            link(pool.affine_select(out=ahead[:], in_=ahead[:], compare_op=ALU.is_ge, fill=FILL, base=P,
                                    pattern=[[-1, T]], channel_multiplier=1))
            pool.iota(slot_id[:], pattern=[[1, P]], base=0, channel_multiplier=0, allow_small_or_imprecise_dtypes=True)
            pool.iota(rev8[:], pattern=[[-1, NE]], base=NE, channel_multiplier=0, allow_small_or_imprecise_dtypes=True)
            pool.memset(half_neg[:], -0.5).then_inc(s["const"], 1)
            link(pool.memset(stage2[:], 0.0))
            pool.dma_start(stage2[0:32, :], ln_g.rearrange("l s (j p) -> (l s j) p", p=P)).then_inc(s["stage2_ld"], 16)
            pool.dma_start(stage2[32:64, :], ln_b.rearrange("l s (j p) -> (l s j) p", p=P)).then_inc(s["stage2_ld"], 16)

            def load_rows(ph):
                l, k = ph // 2, ph % 2
                pool.dma_start(lng_row[:], ln_g[l, k:k + 1, :].broadcast_to([P, D])).then_inc(s["rows_ld"], 16)
                pool.dma_start(lnb_row[:], ln_b[l, k:k + 1, :].broadcast_to([P, D])).then_inc(s["rows_ld"], 16)

            def norm_power(ph):
                for t in range(TT):
                    pool.wait_ge(s["mv"], ph * TT + t + 1)
                    link(pool.tensor_scalar(veps[:, t:t + 1], mv[:, t, 1:2], EPS, None, ALU.add))
                    link(pool.tensor_tensor(rstd[:, t:t + 1], veps[:, t:t + 1], half_neg[:, 0:1], ALU.pow))
                    pool.tensor_scalar(shift_n[:, t:t + 1], mv[:, t, 0:1], rstd[:, t:t + 1], -1.0, ALU.mult, ALU.mult)\
                        .then_inc(s["rstd"], 1)

            for l in range(DEPTH):
                if l:
                    pool.wait_ge(s["x_ln"], 4 * l)
                else:
                    pool.wait_ge(s["mod_sum"], 1)
                load_rows(2 * l)
                pool.dma_start(gnorm[:], gla_norm_g[l:l + 1, :].broadcast_to([P, B_DV])).then_inc(s["wa2_ld"], 16)
                link(pool.memset(wa2[:], 0.0))
                pool.dma_start(wa2[0:RANK, :], w_a2[l]).then_inc(s["wa2_ld"], 16)
                for part in (akP, ikP, qfP, qxP):
                    pool.memset(part[:], 0.0)
                pool.memset(baT[:], 0.0).then_inc(s["pads"], 1)
                for t in range(TT):
                    pool.wait_ge(s["ssq"], l * TT + t + 1)
                    link(pool.tensor_scalar(rms[:, t, :], ssq[:, t, :], 1.0 / B_DV, EPS, ALU.mult, ALU.add))
                    pool.tensor_tensor(rms[:, t, :], rms[:, t, :], half_neg[:, 4:8], ALU.pow).then_inc(s["rms"], 1)
                norm_power(2 * l)
                pool.wait_ge(s["x_ln"], 4 * l + 2)
                if l == 0:
                    load_rows(1)
                    norm_power(1)
            pool.wait_ge(s["r_ps"], 4)
            for z in (hidT_H, hidT_L, d_H, d_L, one_S):
                pool.memset(z[:].bitcast(F32), 0.0)
            pool.memset(hid[:], 0.0).then_inc(s["zeros"], 1)
            pool.wait_ge(s["m_end"], 1)
            load_rows(3)
            norm_power(3)

        def moe_act_down(act, q, it2):
            act.wait_ge(m_ld["d"][q % 2], it2 * (16 * STEPS) + 16 * ((q + 1) // 2 + 1))
            for j in range(2):
                act.wait_ge(s["m_d"], it2 * (4 * STEPS) + (2 * q + j + 3))
                nc.scalar.activation(d_H[:, j, :], raw_d[q % 2][:, j, :], ACT.Copy).then_inc(s["m_dH"], 1)
            act.wait_ge(s["m_t"], it2 * (2 * STEPS) + (q + 3))
            act.wait_ge(s["m_d"], it2 * (4 * STEPS) + (2 * q + 4))
            nc.scalar.activation(hidT_H[:, 0], bank[4][:, 0:256].rearrange("p (a t) -> p a t", a=2), ACT.Copy).then_inc(s["m_tH"], 1)

        @block.scalar
        def _(act):
            A = nc.scalar.activation
            n = [0]

            def link(ins):
                n[0] += 1
                ins.then_inc(s["act_chain"], 1)
                act.wait_ge(s["act_chain"], n[0])

            act.wait_ge(s["cols_rd"], 1)
            A(c_act[:], cols[:, 96:104], ACT.Silu).then_inc(s["cact"], 1)

            def conv_unit(l, u):
                act.wait_ge(w_ld[u % 2], 16 * (l * (9 if u % 2 == 0 else 8) + u // 2 + 1))
                if u >= 2:
                    act.wait_ge(s["proj"], l * NU + u - 1)
                elif l:
                    act.wait_ge(s["f_gu"], 2 * STEPS)
                dst, src = gu_H0[:, :, (u % 2) * 256:(u % 2) * 256 + 256], wraw[u % 2]
                if u in (U_IKW, U_AKV):
                    w = W_IN_UNITS[u][1] - 64
                    A(dst[:, :, 0:128].rearrange("p k (r c) -> p k r c", r=2),
                      src[:, :, 0:64].unsqueeze(2).broadcast_to([P, KT, 2, 64]), ACT.Copy)
                    A(dst[:, :, 128:128 + w], src[:, :, 64:64 + w], ACT.Copy).then_inc(s["wH"], 1)
                else:
                    w = unit_src(l, u)[1]
                    A(dst[:, :, 0:w], src[:, :, 0:w], ACT.Copy).then_inc(s["wH"], 1)

            def evacuate(l, u):
                b = bank[4 + u % 4]
                act.wait_ge(s["proj"], l * NU + u + 1)
                two = b[:].rearrange("p (a t) -> p a t", a=2)
                if u in (U_IQ0, U_IQ1):
                    last = A(iqT[:, 2 * u:2 * u + 2, :], two, ACT.Copy, scale=SQ)
                elif u in (U_AQ0, U_AQ1):
                    v = u - U_AQ0
                    last = A(aqT[:, 2 * v:2 * v + 2, :], two, ACT.Copy, scale=SQ)
                elif u in (U_IKW, U_AKV):
                    act.wait_ge(s["pads"], l + 1)
                    dst = ikP if u == U_IKW else akP
                    A(dst[0:64, 0, :], b[0:64, 0:T], ACT.Copy)
                    last = A(dst[64:128, 1, :], b[64:128, 0:T], ACT.Copy)
                    if u == U_IKW:
                        last = A(iw[:], b[:, T:T + 16].rearrange("p (t h) -> p t h", t=2), ACT.Copy, scale=8 ** -0.5)
                    else:
                        last = A(av[:], b[:, T:T + 128].rearrange("p (t h) -> p t h", t=2), ACT.Copy)
                elif u == U_BQ:
                    last = A(bqT[:], two, ACT.Copy, scale=SQ)
                elif u == U_BK:
                    last = A(bkT[:], two, ACT.Copy)
                elif u == U_BA:
                    last = A(baT[0:RANK, :], b[0:RANK, 0:T], ACT.Copy)
                elif u in (U_BV0, U_BV1):
                    v = u - U_BV0
                    last = A(bv[:, :, v * 256:v * 256 + 256], two, ACT.Copy)
                else:
                    v = u - U_BG0
                    last = A(sbg[:, :, v * 256:v * 256 + 256], two, ACT.Silu)
                last.then_inc(s["evac"], 1)

            def high_of_tokens(ph):
                for h in range(2):
                    act.wait_ge(s["hfull"], ph * KT + 4 * h + 4)
                    A(hT_H[:, 4 * h:4 * h + 4, :], hfull[:, 4 * h:4 * h + 4, :], ACT.Copy).then_inc(s["hT_H"], 1)

            def gate_row(ph, base=4, row=g_row):
                for h in range(2):
                    act.wait_ge(s["g_ps"], 2 * ph + h + 1)
                    A(row[:, h * 512:h * 512 + 512], bank[base + h][:], ACT.Copy).then_inc(s["g_row"], 1)

            def normalise(ph):
                for t in range(TT):
                    act.wait_ge(s["rstd"], TT * ph + t + 1)
                    A(ycat[:, t, :], ycat[:, t, :], ACT.Identity, scale=rstd[:, t:t + 1], bias=shift_n[:, t:t + 1])\
                        .then_inc(s["x_n"], 1)

            def mixer(l):
                conv_unit(l, 0)
                conv_unit(l, 1)
                if l:
                    normalise(2 * l - 1)
                high_of_tokens(2 * l)
                for u in range(NIN):
                    evacuate(l, u)
                    conv_unit(l, u + 2)
                    if u == U_IKW:
                        for k in range(NG):
                            act.wait_ge(s["idx_ps"], l * NG + k + 1)
                            if k >= 2:
                                act.wait_ge(s["idxacc"], l * NG + k - 1)
                            A(relu[k % 2][:], bank[k % 4][:], ACT.Relu).then_inc(s["relu"], 1)
                    if u == U_BV0:
                        act.wait_ge(s["z_ps"], l + 1)
                        for pr in range(2):
                            last = A(dec0[:, pr, :], bank[0][:, pr * T:(pr + 1) * T], ACT.Abs,
                                     bias=cols[:, 104 + 2 * l + pr:105 + 2 * l + pr])
                        link(last)
                        link(A(dec0[:], dec0[:], ACT.Exp, scale=-1.0))
                        A(dec0[:], dec0[:], ACT.Ln, bias=1.0).then_inc(s["az"], 1)
                    if u == U_BV1:
                        act.wait_ge(s["decay"], l + 1)
                        A(dec0[:], dec0[:], ACT.Exp).then_inc(s["qe"], 1)
                        for pr in range(2):
                            A(kx[:, pr, :], bT[:, pr, 0:P], ACT.Exp, scale=-1.0, bias=bT[:, pr, P - 1:P])
                            A(dec1[:, pr, 0:P], bT[:, pr, P:T], ACT.Exp, bias=nb127[:, pr:pr + 1]).then_inc(s["kx_e"], 1)
                        for pr in range(2):
                            act.wait_ge(s["kfac_rd"], 2 * l + pr + 1)
                            A(kfac[:, pr], kfac[:, pr], ACT.Exp).then_inc(s["ke"], 1)
                act.wait_ge(s["at_ps"], 3 * l + 3)
                A(at_sb[:, 2, :], bank[2][:], ACT.Copy).then_inc(s["at_sb"], 1)
                for t in range(TT):
                    act.wait_ge(s["o_ps"], l * TT + t + 1)
                    ob = bank[3] if t == 0 else bank[0]
                    for h in range(B_HEADS):
                        last = A(relu[t][:, h * B_DV:(h + 1) * B_DV], ob[:, h * B_DV:(h + 1) * B_DV], ACT.Square,
                                 accum_out=ssq[:, t, h:h + 1])
                    last.then_inc(s["ssq"], 1)
                for t in range(TT):
                    act.wait_ge(s["nmax"], l * TT + t + 1)
                    for h in range(A_HEADS):
                        last = A(prob[t][:, h, :], prob[t][:, h, :], ACT.Exp, bias=nmax[:, t, h:h + 1],
                                 accum_out=rsum[:, t, h:h + 1])
                    last.then_inc(s["pexp"], 1)
                    for g in range(2) if t == 0 else range(2, NG):
                        act.wait_ge(s["pt_ps"], l * NG + g + 1)
                        dst = pT0[:, 4 * g:4 * g + 4, :] if t == 0 else pT1[:, 4 * (g - 2):4 * (g - 2) + 4, :]
                        A(dst, bank[1 + g % 2][:].rearrange("p (a b) -> p a b", a=4), ACT.Copy).then_inc(s["pt_sb"], 1)
                for b in range(4):
                    act.wait_ge(s["yT_ps"], 4 * l + b + 1)
                    A(hT_H[:, 2 * b:2 * b + 2, :], bank[b][:].rearrange("p (a t) -> p a t", a=2), ACT.Copy)\
                        .then_inc(s["yT_H"], 1)
                for u in range(NIN + 2, NU):
                    conv_unit(l, u)
                    if u == NIN + 2:
                        gate_row(2 * l, 0)

            mixer(0)

            def dense_conv_gu(q):
                if q == 0:
                    act.wait_ge(s["proj"], NU)
                elif q == 1:
                    act.wait_ge(s["yT_L"], 4)
                else:
                    act.wait_ge(s["f_gu"], 2 * (q - 1))
                for i, (k, raw) in enumerate((("g", raw_g), ("u", raw_u))):
                    act.wait_ge(f_ld[k][q % 2], 16 * (q // 2 + 1))
                    A(gu_H[q % 2][:, :, i * FC:(i + 1) * FC], raw[q % 2][:], ACT.Copy).then_inc(s["f_guH"], 1)

            dense_conv_gu(0)
            normalise(0)
            high_of_tokens(1)
            gate_row(1)
            for q in range(STEPS + 1):
                if q + 1 < STEPS:
                    dense_conv_gu(q + 1)
                if q < STEPS:
                    act.wait_ge(s["f_gu"], 2 * q + 1)
                    if q >= 1:
                        act.wait_ge(s["f_hid"], 2 * q - 1)
                    A(silu_g[:, 0, :], bank[0][:, 0:FC], ACT.Silu).then_inc(s["f_silu"], 1)
                if q >= 1:
                    act.wait_ge(f_ld["d"][(q - 1) % 2], 16 * ((q - 1) // 2 + 1))
                    for j in range(2):
                        if q >= 2:
                            act.wait_ge(s["f_d"], 4 * (q - 1))
                        A(d_H[:, j, :], raw_d[(q - 1) % 2][:, j, :], ACT.Copy).then_inc(s["f_dH"], 1)
                    act.wait_ge(s["f_t"], 2 * (q - 1) + 2)
                    if q >= 2:
                        act.wait_ge(s["f_d"], 4 * (q - 1))
                    A(hidT_H[:, 1], bank[7][:, 0:256].rearrange("p (a t) -> p a t", a=2), ACT.Copy).then_inc(s["f_tH"], 1)
                if q < STEPS:
                    act.wait_ge(s["f_gu"], 2 * q + 2)
                    if q >= 1:
                        act.wait_ge(s["f_hid"], 2 * q)
                    A(silu_g[:, 1, :], bank[1][:, 0:FC], ACT.Silu).then_inc(s["f_silu"], 1)
                    act.wait_ge(s["f_t"], 2 * q + 1)
                    if q >= 1:
                        act.wait_ge(s["f_d"], 4 * (q - 1) + 2)
                    A(hidT_H[:, 0], bank[4][:, 0:256].rearrange("p (a t) -> p a t", a=2), ACT.Copy).then_inc(s["f_tH"], 1)

            mixer(1)

            def moe_conv_gu(q, it2):
                if q:
                    act.wait_ge(s["m_gu"], it2 * (2 * STEPS) + q)
                for i, (k, raw) in enumerate((("g", raw_g), ("u", raw_u))):
                    act.wait_ge(m_ld[k][q % 2], it2 * (16 * STEPS) + 16 * (q // 2 + 1))
                    A(gu_H[q % 2][:, :, i * FC:(i + 1) * FC], raw[q % 2][:], ACT.Copy).then_inc(s["m_guH"], 1)

            act.wait_ge(s["proj"], 2 * NU)
            moe_conv_gu(0, 0)
            normalise(2)
            gate_row(3, 1, gate3_row)
            for t in range(TT):
                act.wait_ge(s["xmod"], t + 1)
                A(xH[t][:], ycat[:, t, :], ACT.Copy).then_inc(s["xsplit"], 1)
            act.wait_ge(s["lg8"], 1)
            A(v2[:, 3, :], v2[:, 2, :], ACT.Exp).then_inc(s["expd"], 1)

            def high_gathered(E, b, dst):
                act.wait_ge(s["xg_ps"], E * 2 + (b + 1))
                A(dst[:, 4 * b:4 * b + 4, :], bank[5][:].rearrange("p (k n) -> p k n", k=4), ACT.Copy).then_inc(s["xg_H"], 1)

            def expert_rows(count):
                act.wait_ge(s["m_d"], count)
                for h in range(2):
                    A(yH[:, h * 512:h * 512 + 512], bank[2 + h][:], ACT.Copy).then_inc(s["m_yH"], 1)

            for b in range(2):
                high_gathered(0, b, xgH[0])
            act.wait_ge(s["npass"], 1)
            npass = act.value_load(npass_i[0:1, 0:1], min_val=1, max_val=2)
            with act.Fori(0, npass) as ps:
                with act.Fori(0, NE // 2) as pair:
                    it2 = ps * (NE // 2) + pair
                    for par in range(2):
                        E = it2 * 2 + par
                        for st in range(STEPS):
                            q = par * STEPS + st
                            moe_conv_gu(q + 1, it2)
                            act.wait_ge(s["m_gu"], it2 * (2 * STEPS) + (q + 2))
                            act.wait_ge(s["m_hid"], it2 * (2 * STEPS) + (q + 2))
                            A(silu_g[:, 0, :], bank[q % 2][:, 0:FC], ACT.Silu).then_inc(s["m_silu"], 1)
                            if st == 1:
                                expert_rows(it2 * (4 * STEPS) + (2 * q + 2))
                            moe_act_down(act, q - 1, it2)
                            if st in GATHER_AT:
                                high_gathered(E + 1, GATHER_AT.index(st), xgH[1 - par])
            end2 = npass * (NE // 2)
            moe_act_down(act, -1, end2)
            expert_rows(end2 * (4 * STEPS) + 4)
            normalise(3)

        @block.tensor
        def _(pe):
            mm = nc.tensor.matmul

            def transposed_tokens(src, signal):
                for b in range(4):
                    for i in range(2):
                        for t in range(TT):
                            kt = 2 * b + i
                            last = nc.tensor.transpose(bank[b][:, i * T + t * P:i * T + (t + 1) * P],
                                                       src[:, t, kt * P:(kt + 1) * P], ident[:])
                    last.then_inc(s[signal], 1)

            def gate_row(ph, diag, base=4):
                pe.wait_ge(s["gdiag"], ph + 1)
                for h in range(2):
                    mm(bank[base + h][:], ones[:, 0:P], diag[:, h * 512:(h + 1) * 512], start=True, stop=True)\
                        .then_inc(s["g_ps"], 1)

            pe.wait_ge(s["const"], 1)
            pe.wait_ge(s["stage_ld"], 48)
            nc.tensor.transpose(bank[7][:, 0:P], stage[:], ident[:]).then_inc(s["stageT"], 1)
            pe.wait_ge(s["cact"], 1)
            pe.wait_ge(s["x_ld"], 32)
            transposed_tokens(x_sb, "xT_ps")

            def sum_chunk(acc, o):
                for k in range(KT):
                    last = mm(o[:, k:k + 1], acc[:, k * P:(k + 1) * P], ones[:, 0:1], start=True, stop=True)
                return last
            pe.wait_ge(s["mod_sum"], 1)
            sum_chunk(ycat[:, 0, :], bank[6][:, 0:KT])
            sum_chunk(ycat[:, 1, :], bank[6][:, KT:2 * KT]).then_inc(s["mod_ps"], 1)
            pe.wait_ge(s["stage2_ld"], 32)
            nc.tensor.transpose(bank[7][:, 0:P], stage2[:], ident[:]).then_inc(s["stageT"], 1)

            def project(l, u):
                pe.wait_ge(s["wL"], l * NU + u + 1)
                if u == 3 and l == 0:
                    pe.wait_ge(s["ln_cols"], 1)
                if u == 0:
                    pe.wait_ge(s["hT_L"], 4 * l + 2)
                    if l:
                        pe.wait_ge(s["modT"], 11)
                elif 4 <= u < NIN:
                    pe.wait_ge(s["evac"], l * NIN + u - 3)
                    if l == 0 and u == U_BA + 4:
                        pe.wait_ge(s["modT"], 3)
                elif u == NIN:
                    pe.wait_ge(s["yT_L"], 4 * (l + 1))
                elif u == NIN + 1 and l == 0:
                    pe.wait_ge(s["modT"], 5)
                b = bank[4 + (u % 4 if u < NIN else u - NIN)]
                base = (u % 2) * 256
                if l == 0 and u == U_BA:
                    for a in (2, 3):
                        pe.wait_ge(s["row_rd"], (a - 1) * KT)
                        sum_chunk(mod_acc[a % 2], b[:, T + a * KT:T + (a + 1) * KT]).then_inc(s["mod_ps"], 1)
                WH, WL = gu_H0[:, :, base:base + 256], gu_L0[:, :, base:base + 256]
                if u in (U_BV0, U_BV1, U_BG0, U_BG1) or u >= NIN:
                    for t in range(TT):
                        tok = slice(t * P, (t + 1) * P)
                        for kt in range(KT):
                            last = mm3(b[:, t * 256:(t + 1) * 256], hT_H[:, kt, tok], hT_L[:, kt, tok],
                                       WH[:, kt, :], WL[:, kt, :], kt == 0, kt == KT - 1)
                else:
                    for ct in range(2 if W_IN_UNITS[u][1] == 256 else 1):
                        cc = slice(ct * P, (ct + 1) * P)
                        for kt in range(KT):
                            last = mm3(b[:, ct * T:(ct + 1) * T], WH[:, kt, cc], WL[:, kt, cc],
                                       hT_H[:, kt, :], hT_L[:, kt, :], kt == 0, kt == KT - 1)
                    if u in (U_IKW, U_AKV):
                        w = W_IN_UNITS[u][1] - 64
                        for t in range(TT):
                            tok = slice(t * P, (t + 1) * P)
                            for kt in range(KT):
                                last = mm3(b[:, T + t * w:T + (t + 1) * w], hT_H[:, kt, tok], hT_L[:, kt, tok],
                                           WH[:, kt, P:P + w], WL[:, kt, P:P + w], kt == 0, kt == KT - 1)
                last.then_inc(s["proj"], 1)

            def head_products(l, lhsT, rhs, banks, free, signal):
                for k, (t, heads, keys) in enumerate(HEAD_GROUPS):
                    if k >= 4:
                        pe.wait_ge(s[free], l * NG + k - 3)
                    for i, h in enumerate(heads):
                        last = mm(bank[banks + k % 4][:, i * keys:(i + 1) * keys], lhsT[:, h // 2, t * P:(t + 1) * P],
                                  rhs[:, h % 2, 0:keys], start=True, stop=True)
                    last.then_inc(s[signal], 1)

            def mixer(l):
                if l:
                    pe.wait_ge(s["x_n"], 4 * l)
                    transposed_tokens(ycat, "xT_ps")
                for u in range(NIN):
                    project(l, u)
                    if u == U_AQ0:
                        pe.wait_ge(s["evac"], l * NIN + 3)
                        head_products(l, iqT, ikP, 0, "relu", "idx_ps")
                    if u == U_BV0:
                        pe.wait_ge(s["evac"], l * NIN + 9)
                        pe.wait_ge(s["wa2_ld"], 32 * (l + 1))
                        pe.wait_ge(s["relu"], NG * (l + 1))
                        for pr in range(2):
                            last = mm(bank[0][:, pr * T:(pr + 1) * T], wa2[:, pr * P:(pr + 1) * P], baT[:],
                                      start=True, stop=True)
                        last.then_inc(s["z_ps"], 1)
                pe.wait_ge(s["gla_in"], l + 1)
                for tb in range(2):
                    o = bank[tb][:].rearrange("p (h t) -> p h t", h=4)
                    for pr in range(2):
                        for j in range(NBLK):
                            q0 = j * BLK
                            last = mm(o[:, 2 * pr:2 * pr + 2, q0:q0 + BLK], kfac[:, pr, tb, j, :],
                                      qfP[:, pr, :, tb * P + q0:tb * P + q0 + BLK], start=True, stop=True)
                    last.then_inc(s["at_ps"], 1)
                for pr in range(2):
                    last = mm(bank[2][:, pr * T:(pr + 1) * T], kx[:, pr, :], qxP[:, pr, :, :].rearrange("p a b -> p (a b)"),
                              start=True, stop=True)
                last.then_inc(s["at_ps"], 1)
                pe.wait_ge(s["evac"], NIN * (l + 1))
                head_products(l, aqT, akP, 4, "lg_sb", "lg_ps")
                pe.wait_ge(s["at_msk"], 2 * l + 1)
                for h in range(B_HEADS):
                    e = slice(h * B_DV, (h + 1) * B_DV)
                    last = mm(bank[3][:, e], at_sb[:, 0, e], bv[:, 0, e], start=True, stop=True)
                last.then_inc(s["o_ps"], 1)
                pe.wait_ge(s["at_msk"], 2 * l + 2)
                pe.wait_ge(s["at_sb"], l + 1)
                for h in range(B_HEADS):
                    e = slice(h * B_DV, (h + 1) * B_DV)
                    mm(bank[0][:, e], at_sb[:, 1, e], bv[:, 1, e], start=True, stop=False)
                    last = mm(bank[0][:, e], at_sb[:, 2, e], bv[:, 0, e], start=False, stop=True)
                last.then_inc(s["o_ps"], 1)
                for t in range(TT):
                    pe.wait_ge(s["pexp"], TT * l + t + 1)
                    for g in range(2) if t == 0 else range(2, NG):
                        if g >= 2:
                            pe.wait_ge(s["pt_sb"], l * NG + g - 1)
                        for i in range(4):
                            if t == 0:
                                src = prob0[:, 4 * g + i, :]
                            else:
                                n = 4 * (g - 2) + i
                                src = prob1[:, n // 2, (n % 2) * P:(n % 2 + 1) * P]
                            last = nc.tensor.transpose(bank[1 + g % 2][:, i * P:(i + 1) * P], src, ident[:])
                        last.then_inc(s["pt_ps"], 1)
                    pe.wait_ge(s["pt_sb"], l * NG + (2 if t == 0 else NG))
                    pe.wait_ge(s["lg_sb"], l * NG + 3 + t)
                    for h in range(A_HEADS):
                        e = slice(h * 64, (h + 1) * 64)
                        if t == 0:
                            last = mm(bank[6][:, e], pT0[:, h, :], av[:, 0, :], start=True, stop=True)
                        else:
                            mm(bank[7][:, e], pT1[:, 2 * h, :], av[:, 0, :], start=True, stop=False)
                            last = mm(bank[7][:, e], pT1[:, 2 * h + 1, :], av[:, 1, :], start=False, stop=True)
                    last.then_inc(s["pv_ps"], 1)
                if l == 0:
                    pe.wait_ge(s["lg_sb"], NG)
                    for a in (4, 5):
                        pe.wait_ge(s["row_rd"], (a - 1) * KT)
                        sum_chunk(mod_acc[a % 2], bank[5][:, a * KT:(a + 1) * KT]).then_inc(s["mod_ps"], 1)
                pe.wait_ge(s["ycat"], l + 1)
                transposed_tokens(ycat, "yT_ps")
                for u in range(NIN, NU):
                    project(l, u)
                    if u == NIN:
                        gate_row(2 * l, prob0[:].rearrange("p h t -> p (h t)"), 0)

            def gate_up(b, sH, sL, buf):
                for kt in range(KT):
                    last = mm3(b[:], sH(kt), sL(kt), gu_H[buf][:, kt, :], gu_L[buf][:, kt, :], kt == 0, kt == KT - 1)
                return last

            def hidden_transposes(t, b):
                for j in range(2):
                    last = nc.tensor.transpose(b[:, j * P:(j + 1) * P], hid[:, t, j * P:(j + 1) * P], ident[:])
                return last

            def down(t, j, y, first, last_of_all):
                for h in range(2):
                    cc = slice(h * 512, (h + 1) * 512)
                    last = mm3(y[h][:], hidT_H[:, t, j, :], hidT_L[:, t, j, :], d_H[:, j, cc], d_L[:, j, cc],
                               first, last_of_all)
                return last

            mixer(0)

            pe.wait_ge(s["x_n"], 2)
            transposed_tokens(ycat, "xT_ps")
            gate_row(1, mod_acc[0])
            pe.wait_ge(s["hT_L"], 4)
            pe.wait_ge(s["g_row"], 4)
            ybank = [[bank[2], bank[3]], [bank[5], bank[6]]]
            for q in range(STEPS + 1):
                p = q - 1
                if q < STEPS:
                    pe.wait_ge(s["f_guL"], 2 * (q + 1))
                    if q >= 1:
                        pe.wait_ge(s["f_hid"], 2 * p + 1)
                    gate_up(bank[0], lambda k: hT_H[:, k, 0:P], lambda k: hT_L[:, k, 0:P], q % 2).then_inc(s["f_gu"], 1)
                if q >= 1:
                    pe.wait_ge(s["f_hid"], 2 * p + 2)
                    if q >= 2:
                        pe.wait_ge(s["f_tL"], 2 * p)
                    hidden_transposes(1, bank[7]).then_inc(s["f_t"], 1)
                if q < STEPS:
                    gate_up(bank[1], lambda k: hT_H[:, k, P:T], lambda k: hT_L[:, k, P:T], q % 2).then_inc(s["f_gu"], 1)
                if q >= 1:
                    for t in range(2):
                        pe.wait_ge(s["f_tL"], 2 * p + 1 + t)
                        for j in range(2):
                            pe.wait_ge(s["f_dL"], 2 * p + j + 1)
                            down(t, j, ybank[t], p == 0 and j == 0, p == STEPS - 1 and j == 1).then_inc(s["f_d"], 1)
                if q < STEPS:
                    pe.wait_ge(s["f_hid"], 2 * q + 1)
                    if q in MOD_AT_STEP:
                        a = MOD_AT_STEP[q]
                        pe.wait_ge(s["row_rd"], ROWS_L0 + (a + 1) * KT)
                        pe.wait_ge(s["f_tL"], 2 * q)
                        sum_chunk(mod_acc[a % 2], bank[4][:, T:T + KT]).then_inc(s["mod_ps"], 1)
                    hidden_transposes(0, bank[4]).then_inc(s["f_t"], 1)
            pe.wait_ge(s["row_rd"], len(MOD_ROWS))
            sum_chunk(mod_acc[1], bank[4][:, T:T + KT]).then_inc(s["mod_ps"], 1)

            mixer(1)

            pe.wait_ge(s["x_n"], 6)
            transposed_tokens(ycat, "xT_ps")
            pe.wait_ge(s["rdiag"], 2)
            for i, b in enumerate((4, 5, 6, 3)):
                if i == 3:
                    pe.wait_ge(s["hfull"], 4 * KT)
                mm(bank[b][:], ones[:, 0:P], mod_ring[0][i // 2][:, (i % 2) * 512:(i % 2 + 1) * 512],
                   start=True, stop=True).then_inc(s["r_ps"], 1)
            pe.wait_ge(s["small_ld"], 32)
            for t in range(TT):
                for kt in range(KT):
                    last = mm(bank[7][:, t * NE:(t + 1) * NE], hfull[:, kt, t * P:(t + 1) * P], wr[:, kt, :],
                              start=(kt == 0), stop=(kt == KT - 1))
            last.then_inc(s["rt_ps"], 1)
            gate_row(3, mod_acc[0], 1)
            pe.wait_ge(s["sel"], 1)
            sel = rt[8]
            mm(bank[7][:, 16:24], upper[:], sel[:, 0, :], start=True, stop=True)
            mm(bank[7][:, 24:32], ones[:, 0:P], sel[:, 0, :], start=True, stop=False).then_inc(s["m_gu"], 1)
            mm(bank[7][:, 24:32], upper[:], sel[:, 1, :], start=False, stop=True).then_inc(s["m_t"], 1)
            mm(bank[7][:, 32:40], ones[:, 0:P], sel[:, 0, :], start=True, stop=False)
            mm(bank[7][:, 32:40], ones[:, 0:P], sel[:, 1, :], start=False, stop=True).then_inc(s["rank_ps"], 1)

            def gather(b):
                for i in range(4):
                    kt = 4 * b + i
                    for o, part in ((bank[5], xH), (bank[6], xL)):
                        for t in range(TT):
                            last = mm(o[:, i * P:(i + 1) * P], part[t][:, kt * P:(kt + 1) * P], one_G[:, t, :],
                                      start=(t == 0), stop=(t == TT - 1))
                last.then_inc(s["xg_ps"], 1)

            def scatter(i):
                t, h = i // 2, i % 2
                b = (5, 6, 7, 5)[i]
                tok, cc = slice(t * P, (t + 1) * P), slice(h * 512, (h + 1) * 512)
                mm(bank[b][:], one_S[:, tok], yH[:, cc], start=True, stop=False)
                mm(bank[b][:], one_S[:, tok], yL[:, cc], start=False, stop=True).then_inc(s["m_sc"], 1)

            pe.wait_ge(s["G"], 2)
            pe.wait_ge(s["xsplit"], 2)
            pe.wait_ge(s["xsplitL"], 2)
            gather(0)
            pe.wait_ge(s["xg_H"], 1)
            pe.wait_ge(s["xg_L"], 1)
            gather(1)
            pe.wait_ge(s["zeros"], 1)
            pe.wait_ge(s["g_row"], 2 * DEPTH * 2)
            for b in (2, 3):
                mm(bank[b][:], hidT_H[:, 0, 0, :], d_H[:, 0, 0:512], start=True, stop=False)
            npass = pe.value_load(npass_i[0:1, 0:1], min_val=1, max_val=2)

            def moe_down(q, st, it2):
                pe.wait_ge(s["m_tL"], it2 * (2 * STEPS) + (q + 3))
                for j in range(2):
                    pe.wait_ge(s["m_dL"], it2 * (4 * STEPS) + (2 * q + j + 7))
                    down(0, j, [bank[2], bank[3]], st == 0 and j == 0, st == STEPS - 1 and j == 1)\
                        .then_inc(s["m_d"], 1)

            def moe_transposes(q, it2):
                pe.wait_ge(s["m_hid"], it2 * (2 * STEPS) + (q + 3))
                pe.wait_ge(s["m_tL"], it2 * (2 * STEPS) + (q + 2))
                hidden_transposes(0, bank[4]).then_inc(s["m_t"], 1)

            with pe.Fori(0, npass) as ps:
                with pe.Fori(0, NE // 2) as pair:
                    it2 = ps * (NE // 2) + pair
                    for par in range(2):
                        E = it2 * 2 + par
                        for st in range(STEPS):
                            q = par * STEPS + st
                            if st == 0:
                                pe.wait_ge(s["xg_H"], E * 2 + 2)
                                pe.wait_ge(s["xg_L"], E * 2 + 2)
                            pe.wait_ge(s["m_guL"], it2 * (4 * STEPS) + (2 * q + 6))
                            pe.wait_ge(s["m_hid"], it2 * (2 * STEPS) + (q + 1))
                            gate_up(bank[q % 2], lambda k: xgH[par][:, k, :], lambda k: xgL[par][:, k, :], q % 2)\
                                .then_inc(s["m_gu"], 1)
                            if st == 2:
                                pe.wait_ge(s["m_yL"], E * 2 + 2)
                            if st == 3:
                                pe.wait_ge(s["m_S"], E + 1)
                                for i in range(3):
                                    scatter(i)
                            if st == 4:
                                pe.wait_ge(s["m_acc"], E * 4 + 5)
                                scatter(3)
                                pe.wait_ge(s["m_acc"], E * 4 + 7)
                                for t in range(TT):
                                    last = nc.tensor.transpose(bank[7][:, t * P:(t + 1) * P],
                                                               one_G[:, t, :].bitcast(F32), ident[:])
                                last.then_inc(s["m_st"], 1)
                            if st in GATHER_AT:
                                b = GATHER_AT.index(st)
                                if b == 0:
                                    pe.wait_ge(s["G"], E * 2 + 4)
                                    pe.wait_ge(s["m_acc"], E * 4 + 8)
                                else:
                                    pe.wait_ge(s["xg_H"], E * 2 + 3)
                                    pe.wait_ge(s["xg_L"], E * 2 + 3)
                                gather(b)
                            moe_down(q - 2, (st - 2) % STEPS, it2)
                            moe_transposes(q - 1, it2)
            end2 = npass * (NE // 2)
            n_done = npass * NE
            moe_down(-2, STEPS - 2, end2)
            moe_transposes(-1, end2)
            moe_down(-1, STEPS - 1, end2)
            pe.wait_ge(s["m_yL"], n_done * 2 + 2)
            pe.wait_ge(s["m_S"], n_done + 1)
            for i in range(4):
                if i == 3:
                    pe.wait_ge(s["m_acc"], n_done * 4 + 5)
                else:
                    pe.wait_ge(s["xg_L"], n_done * 2 + 2)
                scatter(i)

        @block.vector
        def _(dve):
            V = nc.vector
            n = [0]

            def link(ins):
                n[0] += 1
                ins.then_inc(s["dve_chain"], 1)
                dve.wait_ge(s["dve_chain"], n[0])

            dve.wait_ge(s["stageT"], 1)
            V.tensor_copy(cols[:], bank[7][:, 0:P]).then_inc(s["cols_rd"], 1)
            dve.wait_ge(s["cols_rd"], 1)

            def conditioning(l, a, o):
                c0 = 48 * l + 8 * a
                return V.scalar_tensor_tensor(out=modT[:, c0:c0 + 8], in0=o, scalar=0.0 if a % 3 == 0 else 1.0,
                                              in1=cols[:, c0:c0 + 8], op0=ALU.add, op1=ALU.add)

            dve.wait_ge(s["cact"], 1)
            for k in range(KT):
                dve.wait_ge(mod_ld[k], 16)
                for a in range(2):
                    w, acc = mod_first[:, k, a * D:(a + 1) * D], ycat[:, a, :]
                    if k == 0:
                        last = V.tensor_scalar(acc, w, c_act[:, 0:1], None, ALU.mult)
                    else:
                        last = V.scalar_tensor_tensor(out=acc, in0=w, scalar=c_act[:, k:k + 1], in1=acc,
                                                      op0=ALU.mult, op1=ALU.add)
                if k < KT - 1:
                    link(last)
            last.then_inc(s["mod_sum"], 1)
            dve.wait_ge(s["mod_ps"], 1)
            for a in range(2):
                last = conditioning(0, a, bank[6][:, a * KT:(a + 1) * KT])
            last.then_inc(s["modT"], 1)
            dve.wait_ge(s["modT"], 1)

            def gate_diag(ph, diag):
                g = modT[:, 48 * (ph // 2) + 16 + 24 * (ph % 2):48 * (ph // 2) + 24 + 24 * (ph % 2)]
                V.tensor_tensor(diag.rearrange("p (k t) -> p k t", k=KT), ident[:].unsqueeze(1).broadcast_to([P, KT, P]),
                                g.unsqueeze(2).broadcast_to([P, KT, P]), ALU.mult).then_inc(s["gdiag"], 1)

            def modulate(ph):
                base = 48 * (ph // 2) + 24 * (ph % 2)
                for kt in range(KT):
                    if ph == 0:
                        scale, shift = modT[:, base + 8 + kt:base + 9 + kt], modT[:, base + kt:base + kt + 1]
                    else:
                        scale, shift = ln_mod[:, ph - 1, 0, kt:kt + 1], ln_mod[:, ph - 1, 1, kt:kt + 1]
                    dve.wait_ge(s["xT_ps"], 4 * ph + kt // 2 + 1)
                    V.tensor_scalar(hfull[:, kt, :], bank[kt // 2][:, (kt % 2) * T:(kt % 2 + 1) * T], scale, shift,
                                    ALU.mult, ALU.add).then_inc(s["hfull"], 1)

            def norm_and_modulation(ph):
                base = 48 * ((ph + 1) // 2) + 24 * ((ph + 1) % 2)
                sc = modT[:, base + 8:base + 16]
                V.tensor_tensor(ln_mod[:, ph, 0, :], ln_cols[:, 8 * ph:8 * ph + 8], sc, ALU.mult)
                link(V.tensor_tensor(ln_mod[:, ph, 1, :], ln_cols[:, 32 + 8 * ph:40 + 8 * ph], sc, ALU.mult))
                link(V.tensor_tensor(ln_mod[:, ph, 1, :], ln_mod[:, ph, 1, :], modT[:, base:base + 8], ALU.add))

            def low_of_tokens(ph):
                for h in range(2):
                    k = slice(4 * h, 4 * h + 4)
                    dve.wait_ge(s["hT_H"], 2 * ph + h + 1)
                    V.tensor_tensor(hT_L[:, k, :], hfull[:, k, :], hT_H[:, k, :].bitcast(F32), ALU.subtract)\
                        .then_inc(s["hT_L"], 1)

            def condition_rows(rows):
                for n in rows:
                    l, a, k = MOD_ROWS[n]
                    row, acc = mod_ring[l][n % 4], mod_acc[a % 2][:]
                    dve.wait_ge(row_ld[n % 4], 16 * (n // 4 + 1))
                    if n:
                        dve.wait_ge(s["row_rd"], n)
                    if k == 0:
                        if l or a >= 4:
                            dve.wait_ge(s["mod_ps"], 4 + a if l else a - 2)
                        last = V.tensor_scalar(acc, row[:], c_act[:, 0:1], None, ALU.mult)
                    else:
                        last = V.scalar_tensor_tensor(out=acc, in0=row[:], scalar=c_act[:, k:k + 1], in1=acc,
                                                      op0=ALU.mult, op1=ALU.add)
                    last.then_inc(s["row_rd"], 1)

            def low_unit(l, u):
                dve.wait_ge(s["wH"], l * NU + u + 1)
                o = (u % 2) * 256
                H, L, src = gu_H0[:, :, o:o + 256], gu_L0[:, :, o:o + 256], wraw[u % 2]
                if u in (U_IKW, U_AKV):
                    w = W_IN_UNITS[u][1] - 64
                    V.tensor_tensor(L[:, :, 0:64], src[:, :, 0:64], H[:, :, 0:64].bitcast(F32), ALU.subtract)
                    V.tensor_tensor(L[:, :, 64:128], src[:, :, 0:64], H[:, :, 64:128].bitcast(F32), ALU.subtract)
                    V.tensor_tensor(L[:, :, 128:128 + w], src[:, :, 64:64 + w], H[:, :, 128:128 + w].bitcast(F32),
                                    ALU.subtract).then_inc(s["wL"], 1)
                else:
                    w = unit_src(l, u)[1]
                    V.tensor_tensor(L[:, :, 0:w], src[:, :, 0:w], H[:, :, 0:w].bitcast(F32), ALU.subtract)\
                        .then_inc(s["wL"], 1)

            def layer_norm(ph, terms):
                dve.wait_ge(s["g_row"], 2 * ph + 2)
                dve.wait_ge(s["rows_ld"], 32 * (ph + 1))
                if ph < 3:
                    norm_and_modulation(ph)
                for t in range(TT):
                    terms(t)
                    link(V.scalar_tensor_tensor(out=ycat[:, t, :], in0=x_sb[:, t, :], scalar=ALPHA, in1=ycat[:, t, :],
                                                op0=ALU.mult, op1=ALU.add))
                    for h in range(2):
                        last = V.bn_stats(stats[:, t, h, :], ycat[:, t, h * 512:(h + 1) * 512])
                    link(last)
                    V.bn_aggr(mv[:, t, :], stats[:, t]).then_inc(s["mv"], 1)
                if ph < 3:
                    modulate(ph + 1)
                    if ph < 2:
                        low_of_tokens(ph + 1)

            def norm_out(ph):
                for t in range(TT):
                    dve.wait_ge(s["x_n"], TT * ph + t + 1)
                    link(V.tensor_tensor(x_sb[:, t, :], ycat[:, t, :], lng_row[:], ALU.mult))
                    V.tensor_tensor(x_sb[:, t, :], x_sb[:, t, :], lnb_row[:], ALU.add).then_inc(s["x_ln"], 1)

            def indexer(l):
                for k, (t, heads, keys) in enumerate(HEAD_GROUPS):
                    dve.wait_ge(s["relu"], l * NG + k + 1)
                    for i, h in enumerate(heads):
                        src = relu[k % 2][:, i * keys:(i + 1) * keys]
                        if h == 0:
                            last = V.tensor_scalar(score[t][:], src, iw[:, t, h:h + 1], None, ALU.mult)
                        else:
                            last = V.scalar_tensor_tensor(out=score[t][:], in0=src, scalar=iw[:, t, h:h + 1],
                                                          in1=score[t][:], op0=ALU.mult, op1=ALU.add)
                        if i < len(heads) - 1:
                            link(last)
                    last.then_inc(s["idxacc"], 1)
                    dve.wait_ge(s["idxacc"], l * NG + k + 1)
                for t in range(TT):
                    last = V.tensor_tensor(score[t][:], score[t][:], ahead[:, P:T] if t == 0 else ahead[:], ALU.add)
                link(last)

            def select(t):
                for _ in range(TOPK // 8):
                    link(V.max(top8[:], score[t][:]))
                    link(V.match_replace(score[t][:], top8[:], score[t][:], -3.4e38))
                link(V.tensor_scalar(score[t][:], score[t][:], TAKEN, NEG, ALU.is_gt, ALU.mult))
                link(V.tensor_tensor(dsel[t][:], score[t][:], dist[:, P:T] if t == 0 else dist[:], ALU.add))

            def decay(l):
                dve.wait_ge(s["z_ps"], l + 1)
                dve.wait_ge(s["az"], l + 1)
                for pr in range(2):
                    last = V.tensor_scalar(dec1[:, pr, :], bank[0][:, pr * T:(pr + 1) * T],
                                           cols[:, 104 + 2 * l + pr:105 + 2 * l + pr], 0.0, ALU.add, ALU.min)
                link(last)
                link(V.tensor_tensor(dec1[:], dec1[:], dec0[:], ALU.subtract))
                link(V.tensor_scalar(dec1[:], dec1[:], 1.0 / 16.0, None, ALU.mult))
                for pr in range(2):
                    last = V.tensor_tensor_scan(bT[:, pr, :], ones[:], dec1[:, pr, :], 0.0, ALU.mult, ALU.add)
                link(last)
                V.tensor_scalar(nb127[:], bT[:, :, P - 1], -1.0, None, ALU.mult)
                blocks = bT[:].rearrange("p a (j b) -> p (a j) b", b=BLK)
                mid = blocks[:, :, BLK // 2:BLK // 2 + 1]
                V.tensor_tensor(dec0[:].rearrange("p a (j b) -> p (a j) b", b=BLK), blocks,
                                mid.broadcast_to([P, 2 * T // BLK, BLK]), ALU.subtract).then_inc(s["decay"], 1)
                for pr in range(2):
                    b = bT[:, pr, :].rearrange("p (a n) -> p a n", a=2)
                    r = bT[:, pr, :].rearrange("p (a j b) -> p a j b", a=2, b=BLK)[:, :, :, BLK // 2:BLK // 2 + 1]
                    link(V.tensor_tensor(kfac[:, pr], r.broadcast_to([P, 2, NBLK, P]),
                                         b.unsqueeze(2).broadcast_to([P, 2, NBLK, P]), ALU.subtract))
                    V.tensor_scalar(kfac[:, pr], kfac[:, pr], 40.0, None, ALU.min).then_inc(s["kfac_rd"], 1)

            def decay_products(l):
                dve.wait_ge(s["evac"], l * NIN + U_BK + 1)
                dve.wait_ge(s["pads"], l + 1)
                dve.wait_ge(s["qe"], l + 1)
                dve.wait_ge(s["kx_e"], 2 * l + 2)
                for h in range(2):
                    p = slice(64 * h, 64 * h + 64)
                    V.tensor_tensor(qfP[p, :, h, :], bqT[p, :, :], dec0[p, :, :], ALU.mult)
                    V.tensor_tensor(qxP[p, :, h, :], bqT[p, :, P:T], dec1[p, :, 0:P], ALU.mult)
                V.tensor_tensor(kx[:], kx[:], bkT[:, :, 0:P], ALU.mult)
                for pr in range(2):
                    dve.wait_ge(s["ke"], 2 * l + pr + 1)
                    k = bkT[:, pr, :].rearrange("p (a n) -> p a n", a=2).unsqueeze(2).broadcast_to([P, 2, NBLK, P])
                    last = V.tensor_tensor(kfac[:, pr], kfac[:, pr], k, ALU.mult)
                last.then_inc(s["gla_in"], 1)

            def mixer(l):
                ph = 2 * l
                if l == 0:
                    modulate(ph)
                    low_of_tokens(ph)
                for u in range(NIN + 2):
                    low_unit(l, u)
                    if u == 1 and l == 0:
                        dve.wait_ge(s["stageT"], 2)
                        V.tensor_copy(ln_cols[:], bank[7][:, 0:64]).then_inc(s["ln_cols"], 1)
                        dve.wait_ge(s["ln_cols"], 1)
                    elif u == 1:
                        norm_out(1)
                    if l == 0:
                        condition_rows(unit_rows(u))
                    if l == 0 and u == U_BA + 2:
                        dve.wait_ge(s["evac"], U_BA + 1)
                        for a in (2, 3):
                            conditioning(0, a, bank[4 + U_BA % 4][:, T + a * KT:T + (a + 1) * KT]).then_inc(s["modT"], 1)
                    if u == U_AQ1:
                        dve.wait_ge(s["evac"], l * NIN + 3)
                        indexer(l)
                    if u == U_AKV:
                        select(0)
                    if u == U_BQ:
                        select(1)
                    if u == U_BG0:
                        decay(l)
                    if u == U_BG1:
                        decay_products(l)
                for tb in range(2):
                    dve.wait_ge(s["at_ps"], 3 * l + tb + 1)
                    V.tensor_tensor(at_sb[:, tb, :].rearrange("p (h t) -> p h t", h=4),
                                    bank[tb][:].rearrange("p (h t) -> p h t", h=4),
                                    upper_eq[:].unsqueeze(1).broadcast_to([P, 4, P]), ALU.mult).then_inc(s["at_msk"], 1)
                for k, (t, heads, keys) in enumerate(HEAD_GROUPS):
                    dve.wait_ge(s["lg_ps"], l * NG + k + 1)
                    for i, h in enumerate(heads):
                        last = V.scalar_tensor_tensor(out=prob[t][:, h, :], in0=dsel[t][:], scalar=2.0 ** -(h + 1),
                                                      in1=bank[4 + k % 4][:, i * keys:(i + 1) * keys],
                                                      op0=ALU.mult, op1=ALU.add)
                    last.then_inc(s["lg_sb"], 1)
                    if k in (1, NG - 1):
                        dve.wait_ge(s["lg_sb"], l * NG + k + 1)
                        V.tensor_reduce(nmax[:, t, :], prob[t][:], AX.X, ALU.max, negate=True).then_inc(s["nmax"], 1)
                dve.wait_ge(s["evac"], l * NIN + NIN)
                dve.wait_ge(s["wa2_ld"], 32 * (l + 1))
                for t in range(TT):
                    g = sbg[:, t, :].rearrange("p (h e) -> p h e", h=B_HEADS)
                    last = V.tensor_tensor(g, g, gnorm[:].unsqueeze(1).broadcast_to([P, B_HEADS, B_DV]), ALU.mult)
                link(last)
                for t in range(TT):
                    ob = bank[3] if t == 0 else bank[0]
                    dve.wait_ge(s["rms"], l * TT + t + 1)
                    for h in range(B_HEADS):
                        e = slice(h * B_DV, (h + 1) * B_DV)
                        V.scalar_tensor_tensor(out=ycat[:, t, 512 + h * B_DV:512 + (h + 1) * B_DV], in0=ob[:, e],
                                               scalar=rms[:, t, h:h + 1], in1=sbg[:, t, e], op0=ALU.mult, op1=ALU.mult)
                for t in range(TT):
                    dve.wait_ge(s["pv_ps"], l * TT + t + 1)
                    link(V.reciprocal(rinv[:, t, :], rsum[:, t, :]))
                    last = V.tensor_tensor(ycat[:, t, 0:512].rearrange("p (h e) -> p h e", h=A_HEADS),
                                           bank[6 + t][:].rearrange("p (h e) -> p h e", h=A_HEADS),
                                           rinv[:, t, :].unsqueeze(2).broadcast_to([P, A_HEADS, 64]), ALU.mult)
                last.then_inc(s["ycat"], 1)
                if l == 0:
                    dve.wait_ge(s["mod_ps"], 5)
                    for a in (4, 5):
                        conditioning(0, a, bank[5][:, a * KT:(a + 1) * KT]).then_inc(s["modT"], 1)
                for b in range(4):
                    dve.wait_ge(s["yT_H"], 4 * l + b + 1)
                    k = slice(2 * b, 2 * b + 2)
                    V.tensor_tensor(hT_L[:, k, :], bank[b][:].rearrange("p (a t) -> p a t", a=2),
                                    hT_H[:, k, :].bitcast(F32), ALU.subtract).then_inc(s["yT_L"], 1)
                dve.wait_ge(s["modT"], 5 if l == 0 else 11)
                gate_diag(ph, prob0[:].rearrange("p h t -> p (h t)"))
                if l == 0:
                    gate_diag(1, mod_acc[0][:])
                else:
                    for i, a in enumerate((4, 3)):
                        V.tensor_tensor(mod_ring[0][i][:].rearrange("p (k t) -> p k t", k=KT),
                                        ident[:].unsqueeze(1).broadcast_to([P, KT, P]),
                                        modT[:, 48 + 8 * a:56 + 8 * a].unsqueeze(2).broadcast_to([P, KT, P]), ALU.mult)\
                            .then_inc(s["rdiag"], 1)
                    gate_diag(3, mod_acc[0][:])
                for u in range(NIN + 2, NU):
                    low_unit(l, u)

                def terms(t):
                    for v in range(4):
                        if t == 0:
                            dve.wait_ge(s["proj"], l * NU + NIN + v + 1)
                        cc = slice(v * 256, (v + 1) * 256)
                        last = V.tensor_tensor(ycat[:, t, cc], bank[4 + v][:, t * 256:(t + 1) * 256], g_row[:, cc], ALU.mult)
                    link(last)
                layer_norm(ph, terms)

            mixer(0)

            def dense_low_gu(q):
                for i, raw in enumerate((raw_g, raw_u)):
                    cc = slice(i * FC, (i + 1) * FC)
                    dve.wait_ge(s["f_guH"], 2 * q + i + 1)
                    V.tensor_tensor(gu_L[q % 2][:, :, cc], raw[q % 2][:], gu_H[q % 2][:, :, cc].bitcast(F32), ALU.subtract)\
                        .then_inc(s["f_guL"], 1)

            dense_low_gu(0)
            for q in range(STEPS + 1):
                p = q - 1
                if q + 1 < STEPS:
                    dense_low_gu(q + 1)
                if q < STEPS:
                    dve.wait_ge(s["f_silu"], 2 * q + 1)
                    if q >= 1:
                        dve.wait_ge(s["f_t"], 2 * p + 1)
                    V.tensor_tensor(hid[:, 0, :], silu_g[:, 0, :], bank[0][:, FC:2 * FC], ALU.mult).then_inc(s["f_hid"], 1)
                if q == 0:
                    norm_out(0)
                if q >= 1:
                    for j in range(2):
                        dve.wait_ge(s["f_dH"], 2 * p + j + 1)
                        V.tensor_tensor(d_L[:, j, :], raw_d[p % 2][:, j, :], d_H[:, j, :].bitcast(F32), ALU.subtract)\
                            .then_inc(s["f_dL"], 1)
                    dve.wait_ge(s["f_tH"], 2 * p + 2)
                    V.tensor_tensor(hidT_L[:, 1], bank[7][:, 0:256].rearrange("p (a t) -> p a t", a=2),
                                    hidT_H[:, 1].bitcast(F32), ALU.subtract).then_inc(s["f_tL"], 1)
                if q < STEPS:
                    dve.wait_ge(s["f_silu"], 2 * q + 2)
                    if q >= 1:
                        dve.wait_ge(s["f_t"], 2 * p + 2)
                    V.tensor_tensor(hid[:, 1, :], silu_g[:, 1, :], bank[1][:, FC:2 * FC], ALU.mult).then_inc(s["f_hid"], 1)
                    condition_rows(step_rows(q))
                    dve.wait_ge(s["f_tH"], 2 * q + 1)
                    if q in MOD_AT_STEP:
                        conditioning(1, MOD_AT_STEP[q], bank[4][:, T:T + KT]).then_inc(s["modT"], 1)
                    V.tensor_tensor(hidT_L[:, 0], bank[4][:, 0:256].rearrange("p (a t) -> p a t", a=2),
                                    hidT_H[:, 0].bitcast(F32), ALU.subtract).then_inc(s["f_tL"], 1)

            def dense_terms(t):
                dve.wait_ge(s["f_d"], 4 * STEPS - (2 if t == 0 else 0))
                for h in range(2):
                    cc = slice(h * 512, (h + 1) * 512)
                    last = V.tensor_tensor(ycat[:, t, cc], bank[(2, 5)[t] + h][:], g_row[:, cc], ALU.mult)
                link(last)
            dve.wait_ge(s["mod_ps"], 11)
            conditioning(1, 5, bank[4][:, T:T + KT]).then_inc(s["modT"], 1)
            layer_norm(1, dense_terms)

            mixer(1)

            V.memset(tick[:, 0:1], 0.0).then_inc(s["m_guL"], 4)
            V.memset(tick[:, 1:2], 0.0).then_inc(s["m_dL"], 4)
            V.memset(tick[:, 2:3], 0.0).then_inc(s["m_hid"], 2)
            V.memset(tick[:, 3:4], 0.0).then_inc(s["m_tL"], 1)
            V.memset(tick[:, 5:6], 0.0).then_inc(s["m_S"], 1)
            norm_out(2)
            dve.wait_ge(s["rt_ps"], 1)
            dve.wait_ge(s["small_ld"], 32)
            lg, cand, oh1, lg2, oh2, tmp, gate = rt[0], rt[1], rt[2], rt[3], rt[4], rt[5], rt[6]
            rank, sel, rank_m = rt[7], rt[8], rt[9]

            def wide(v):
                return v.unsqueeze(2).broadcast_to([P, TT, NE])
            rev = rev8[:].unsqueeze(1).broadcast_to([P, TT, NE])
            link(V.tensor_tensor(lg[:], bank[7][:, 0:16].rearrange("p (t e) -> p t e", t=2),
                                 br_row[:].unsqueeze(1).broadcast_to([P, TT, NE]), ALU.add))

            def first_highest(src, value, mark):
                link(V.tensor_reduce(value, src[:], AX.X, ALU.max))
                link(V.tensor_tensor(cand[:], src[:], wide(value), ALU.is_equal))
                link(V.tensor_tensor(cand[:], cand[:], rev, ALU.mult))
                link(V.tensor_reduce(v2[:, 5, :], cand[:], AX.X, ALU.max))
                link(V.tensor_tensor(mark[:], cand[:], wide(v2[:, 5, :]), ALU.is_equal))
            first_highest(lg, v2[:, 0, :], oh1)
            link(V.scalar_tensor_tensor(out=lg2[:], in0=oh1[:], scalar=FILL, in1=lg[:], op0=ALU.mult, op1=ALU.add))
            first_highest(lg2, v2[:, 1, :], oh2)
            V.tensor_tensor(sel[:], oh1[:], oh2[:], ALU.add).then_inc(s["sel"], 1)
            V.tensor_tensor(v2[:, 2, :], v2[:, 1, :], v2[:, 0, :], ALU.subtract).then_inc(s["lg8"], 1)
            dve.wait_ge(s["r_ps"], 4)
            dve.wait_ge(s["x_ln"], 6)
            for t in range(TT):
                for i, b in enumerate((4, 5)):
                    cc = slice(i * 512, (i + 1) * 512)
                    last = V.tensor_tensor(ycat[:, t, cc], x_sb[:, t, cc], bank[b][:], ALU.mult)
                link(last)
                for i, b in enumerate((6, 3)):
                    cc = slice(i * 512, (i + 1) * 512)
                    last = V.tensor_tensor(ycat[:, t, cc], ycat[:, t, cc], bank[b][:], ALU.add)
                last.then_inc(s["xmod"], 1)
            dve.wait_ge(s["sel"], 1)
            dve.wait_ge(s["rank_ps"], 1)
            link(V.tensor_scalar(rank[:], bank[7][:, 16:32].rearrange("p (t e) -> p t e", t=2), 1.0, None, ALU.add))
            link(V.tensor_tensor(rank_m[:], rank[:], sel[:], ALU.mult))
            link(V.memset(rank_tab[:], -1.0))
            V.tensor_scalar(rank_tab[:, :, 0:NE], rank_m[:], -1.0, None, ALU.add)
            link(V.tensor_scalar(rank_tab[:, :, NE:2 * NE], rank_m[:], -1.0 - P, None, ALU.add))
            link(V.tensor_reduce(npass_f[:, 0:1], bank[7][:, 32:40], AX.X, ALU.max))
            link(V.tensor_scalar(npass_f[:, 1:2], npass_f[:, 0:1], float(P), 1.0, ALU.is_gt, ALU.add))
            V.tensor_copy(npass_i[:], npass_f[:, 1:2]).then_inc(s["npass"], 1)

            def one_hot(col):
                for t in range(TT):
                    V.tensor_scalar(one_G[:, t, :], slot_id[:], rank_tab[:, t, col], None, ALU.is_equal).then_inc(s["G"], 1)
            one_hot(slice(0, 1))
            for t in range(TT):
                dve.wait_ge(s["xsplit"], t + 1)
                last = V.tensor_tensor(xL[t][:], ycat[:, t, :], xH[t][:].bitcast(F32), ALU.subtract)
                last.then_inc(s["xsplitL"], 1)

            dve.wait_ge(s["expd"], 1)
            link(V.tensor_scalar(v2[:, 4, :], v2[:, 3, :], 1.0, None, ALU.add))
            link(V.reciprocal(v2[:, 0, :], v2[:, 4, :]))
            link(V.tensor_tensor(v2[:, 1, :], v2[:, 3, :], v2[:, 0, :], ALU.mult))
            V.tensor_tensor(tmp[:], oh1[:], wide(v2[:, 0, :]), ALU.mult)
            link(V.tensor_tensor(gate[:], oh2[:], wide(v2[:, 1, :]), ALU.mult))
            link(V.memset(gate_tab[:], 0.0))
            for p in range(2):
                last = V.tensor_tensor(gate_tab[:, :, 1 + p * NE:1 + (p + 1) * NE], gate[:], tmp[:], ALU.add)
            dve.wait_ge(s["xsplitL"], 2)
            V.memset(ycat[:], 0.0).then_inc(s["m_acc"], 4)

            def moe_low_gu(q, it2):
                for i, raw in enumerate((raw_g, raw_u)):
                    cc = slice(i * FC, (i + 1) * FC)
                    dve.wait_ge(s["m_guH"], it2 * (4 * STEPS) + (2 * q + i + 1))
                    V.tensor_tensor(gu_L[q % 2][:, :, cc], raw[q % 2][:], gu_H[q % 2][:, :, cc].bitcast(F32), ALU.subtract)\
                        .then_inc(s["m_guL"], 1)

            def low_gathered(E, b, dst):
                dve.wait_ge(s["xg_ps"], E * 2 + (b + 1))
                V.tensor_copy(dst[:, 4 * b:4 * b + 4, :], bank[6][:].rearrange("p (k n) -> p k n", k=4)).then_inc(s["xg_L"], 1)

            def moe_low_down(q, it2):
                for j in range(2):
                    dve.wait_ge(s["m_dH"], it2 * (4 * STEPS) + (2 * q + j + 3))
                    V.tensor_tensor(d_L[:, j, :], raw_d[q % 2][:, j, :], d_H[:, j, :].bitcast(F32), ALU.subtract)\
                        .then_inc(s["m_dL"], 1)
                dve.wait_ge(s["m_tH"], it2 * (2 * STEPS) + (q + 2))
                V.tensor_tensor(hidT_L[:, 0], bank[4][:, 0:256].rearrange("p (a t) -> p a t", a=2),
                                hidT_H[:, 0].bitcast(F32), ALU.subtract).then_inc(s["m_tL"], 1)

            def expert_rows(E):
                for h in range(2):
                    dve.wait_ge(s["m_yH"], E * 2 + (h + 1))
                    cc = slice(h * 512, (h + 1) * 512)
                    V.tensor_tensor(yL[:, cc], bank[2 + h][:], yH[:, cc].bitcast(F32), ALU.subtract).then_inc(s["m_yL"], 1)

            def accumulate(E, quarters):
                for i in quarters:
                    t, h = i // 2, i % 2
                    a = ycat[:, t, h * 512:(h + 1) * 512]
                    dve.wait_ge(s["m_sc"], E * 4 + (i + 1))
                    if i == 0:
                        dve.wait_ge(s["m_acc"], E * 4 + 4)
                    V.scalar_tensor_tensor(out=a, in0=bank[(5, 6, 7, 5)[i]][:], scalar=gate_tab[:, t, bass.ds(E, 1)],
                                           in1=a, op0=ALU.mult, op1=ALU.add).then_inc(s["m_acc"], 1)

            moe_low_gu(0, 0)
            for b in range(2):
                low_gathered(0, b, xgL[0])
            dve.wait_ge(s["npass"], 1)
            npass = dve.value_load(npass_i[0:1, 0:1], min_val=1, max_val=2)
            with dve.Fori(0, npass) as ps:
                with dve.Fori(0, NE // 2) as pair:
                    it2 = ps * (NE // 2) + pair
                    for par in range(2):
                        E = it2 * 2 + par
                        for st in range(STEPS):
                            q = par * STEPS + st
                            moe_low_gu(q + 1, it2)
                            dve.wait_ge(s["m_silu"], it2 * (2 * STEPS) + (q + 1))
                            dve.wait_ge(s["m_t"], it2 * (2 * STEPS) + (q + 2))
                            V.tensor_tensor(hid[:, 0, :], silu_g[:, 0, :], bank[q % 2][:, FC:2 * FC], ALU.mult)\
                                .then_inc(s["m_hid"], 1)
                            if st == 1:
                                expert_rows(E)
                            moe_low_down(q - 1, it2)
                            if st == 3:
                                accumulate(E, range(3))
                            if st == 4:
                                accumulate(E, range(3, 4))
                            if st == 5:
                                dve.wait_ge(s["m_st"], E + 1)
                                V.tensor_copy(one_S[:], bank[7][:, 0:T]).then_inc(s["m_S"], 1)
                                one_hot(bass.ds(E + 1, 1))
                            if st in GATHER_AT:
                                low_gathered(E + 1, GATHER_AT.index(st), xgL[1 - par])
            n_done = npass * NE
            dve.wait_ge(s["xg_L"], n_done * 2 + 2)
            V.memset(tick[:, 6:7], 0.0).then_inc(s["m_end"], 1)
            moe_low_down(-1, npass * (NE // 2))
            expert_rows(n_done)
            accumulate(n_done, range(4))
            dve.wait_ge(s["m_acc"], n_done * 4 + 8)

            def moe_terms(t):
                link(V.tensor_tensor(ycat[:, t, :], ycat[:, t, :], gate3_row[:], ALU.mult))
            layer_norm(3, moe_terms)
            norm_out(3)


_INS = ["x", "c", "w_in", "w_a2", "b_a", "gla_norm_g", "w_out", "w_mod", "b_mod", "ln_g", "ln_b",
        "ffn_w_gate", "ffn_w_up", "ffn_w_down", "w_router", "b_router", "moe_w_gate", "moe_w_up", "moe_w_down"]
_OUTS = [((1, T, D), "float32")]


def kernel(**inputs):
    import numpy as np
    import concourse.bacc as bacc
    from concourse.bass_utils import run_bass_kernel_spmd

    nc = bacc.Bacc("TRN2", target_bir_lowering=False, num_devices=1)
    arrays, args = {}, []
    for name in _INS:
        a = np.ascontiguousarray(inputs[name])
        arrays[f"in_{name}_dram"] = a
        args.append(nc.dram_tensor(f"in_{name}_dram", a.shape, mybir.dt.from_np(a.dtype), kind="ExternalInput").ap())
    for i, (shape, dtype) in enumerate(_OUTS):
        args.append(nc.dram_tensor(f"out_{i}_dram", shape, mybir.dt.from_np(np.dtype(dtype)), kind="ExternalOutput").ap())
    hybrid_decoder(nc, *args)
    r = run_bass_kernel_spmd(nc, [arrays], core_ids=[0])
    return r.results[0]["out_0_dram"]
```
